# Optimizing a Trainium2 kernel written in Bass

```python
import math
import jax, jax.numpy as jnp
from jax import lax
import numpy as np

D_MODEL = 2048
BATCH = 1
SEQ = 256
DEPTH = 1

ATTN_HEADS = 16
ATTN_HEAD_DIM = 128
ATTN_W = ATTN_HEADS * ATTN_HEAD_DIM
SSM_HEADS = 32
SSM_HEAD_DIM = 64
SSM_W = SSM_HEADS * SSM_HEAD_DIM
MIX_W = ATTN_W + SSM_W
SSM_GROUPS = 8
SSM_HEADS_PER_GROUP = SSM_HEADS // SSM_GROUPS
SSM_STATE = 128
CONV_WIDTH = 5
CONV_DIM = SSM_W + 2 * SSM_GROUPS * SSM_STATE
CHUNK = 128
IN_W = 3 * ATTN_W + SSM_W + CONV_DIM + 2 * SSM_HEADS
DILATED_PATTERNS = ((128, 1), (512, 4), (2048, 16))
BLK = 64
NUM_BUCKETS = 32
MAX_DISTANCE = 1024
NEG_INF = -1e30
D_FF = 4 * D_MODEL
EPS = 1e-6

kernel_name = "hybrid_dilated_attn_ssd_block"

def rms_norm(x, g):
    xf = x.astype(jnp.float32)
    y = xf * lax.rsqrt(jnp.mean(xf * xf, axis=-1, keepdims=True) + EPS)
    return (y * g.astype(jnp.float32)).astype(x.dtype)

def t5_bucket(rel):
    nb = NUM_BUCKETS // 2
    max_exact = nb // 2
    ret = (rel > 0).astype(jnp.int32) * nb
    n = jnp.abs(rel)
    nf = jnp.maximum(n, 1).astype(jnp.float32)
    large = max_exact + (jnp.log(nf / max_exact) / math.log(MAX_DISTANCE / max_exact)
                         * (nb - max_exact)).astype(jnp.int32)
    large = jnp.minimum(large, nb - 1)
    return ret + jnp.where(n < max_exact, n, large)

def dilated_window_attention(q, k, v, rel_bias, window, dilation):
    b, S, H, e = q.shape
    half = window // (2 * dilation)
    L = S // dilation
    nb = -(-L // BLK)
    Lp = nb * BLK

    def to_sub(t):
        t = t.reshape(b, L, dilation, H, e).transpose(0, 2, 3, 1, 4)
        return jnp.pad(t, ((0, 0), (0, 0), (0, 0), (0, Lp - L), (0, 0)))

    def windows(t):
        tp = jnp.pad(to_sub(t), ((0, 0), (0, 0), (0, 0), (BLK, BLK), (0, 0)))
        tp = tp.reshape(b, dilation, H, nb + 2, BLK, e)
        return jnp.concatenate([tp[:, :, :, :-2], tp[:, :, :, 1:-1], tp[:, :, :, 2:]], axis=-2)

    qs = to_sub(q).reshape(b, dilation, H, nb, BLK, e)
    kw, vw = windows(k), windows(v)

    s_idx = jnp.arange(BLK)[:, None]
    t_idx = jnp.arange(3 * BLK)[None, :]
    rel = t_idx - BLK - s_idx
    bias = rel_bias[t5_bucket(rel * dilation)].transpose(2, 0, 1)
    key_pos = jnp.arange(nb)[:, None] * BLK + t_idx - BLK
    valid = (jnp.abs(rel) <= half)[None] & ((key_pos >= 0) & (key_pos < L))[:, None, :]

    scale = 1.0 / math.sqrt(e)
    logits = jnp.einsum('bdhnqe,bdhnke->bdhnqk', qs, kw).astype(jnp.float32) * scale
    logits = logits + bias[:, None].astype(jnp.float32)
    logits = jnp.where(valid, logits, NEG_INF)
    m = jnp.max(logits, axis=-1, keepdims=True)
    p = jnp.exp(logits - m)
    den = jnp.sum(p, axis=-1)
    o = jnp.einsum('bdhnqk,bdhnke->bdhnqe', p, vw.astype(jnp.float32)) / den[..., None]
    lse = m[..., 0] + jnp.log(den)

    o = o.reshape(b, dilation, H, Lp, e)[:, :, :, :L].transpose(0, 3, 1, 2, 4).reshape(b, S, H, e)
    lse = lse.reshape(b, dilation, H, Lp)[:, :, :, :L].transpose(0, 3, 1, 2).reshape(b, S, H)
    return o, lse

def segsum(a):
    T = a.shape[-1]
    cs = jnp.cumsum(a, axis=-1)
    diff = cs[..., :, None] - cs[..., None, :]
    return jnp.where(jnp.tril(jnp.ones((T, T), dtype=bool)), diff, -jnp.inf)

def ssd_chunked(x, dt, A, Bm, Cm):
    b, L, g, h, p = x.shape
    n = Bm.shape[-1]
    nc = L // CHUNK
    xc = (x.astype(jnp.float32) * dt[..., None]).reshape(b, nc, CHUNK, g, h, p)
    Bc = Bm.reshape(b, nc, CHUNK, g, n)
    Cc = Cm.reshape(b, nc, CHUNK, g, n)
    ac = (dt * A).reshape(b, nc, CHUNK, g, h).transpose(0, 3, 4, 1, 2)
    a_cum = jnp.cumsum(ac, axis=-1)

    Lmat = jnp.exp(segsum(ac))
    cb = jnp.einsum('bclgn,bcsgn->bgcls', Cc, Bc)
    y_diag = jnp.einsum('bgcls,bghcls,bcsghp->bclghp', cb, Lmat, xc)

    decay_states = jnp.exp(a_cum[..., -1:] - a_cum)
    states = jnp.einsum('bclgn,bghcl,bclghp->bcghpn', Bc, decay_states, xc)
    states = jnp.concatenate([jnp.zeros_like(states[:, :1]), states], axis=1)

    a_last = jnp.pad(a_cum[..., -1], ((0, 0), (0, 0), (0, 0), (1, 0)))
    chunk_decay = jnp.exp(segsum(a_last))
    states = jnp.einsum('bghzc,bcghpn->bzghpn', chunk_decay, states)[:, :-1]

    y_off = jnp.einsum('bclgn,bcghpn,bghcl->bclghp', Cc, states, jnp.exp(a_cum))
    return (y_diag + y_off).reshape(b, L, g, h, p).astype(x.dtype)

def ssd_mixer(z, xbc, dt_raw, conv_w, conv_b, dt_bias, a_log, d_skip, norm_g):
    b, S, _ = xbc.shape
    pad = CONV_WIDTH // 2
    xbc = lax.conv_general_dilated(xbc, conv_w[:, None, :], window_strides=(1,),
                                   padding=[(pad, pad)], dimension_numbers=('NWC', 'WIO', 'NWC'),
                                   feature_group_count=CONV_DIM) + conv_b
    xbc = jax.nn.silu(xbc)
    gn = SSM_GROUPS * SSM_STATE
    xs = xbc[..., :SSM_W].reshape(b, S, SSM_GROUPS, SSM_HEADS_PER_GROUP, SSM_HEAD_DIM)
    Bm = xbc[..., SSM_W:SSM_W + gn].reshape(b, S, SSM_GROUPS, SSM_STATE)
    Cm = xbc[..., SSM_W + gn:].reshape(b, S, SSM_GROUPS, SSM_STATE)

    dt = jax.nn.softplus(dt_raw.astype(jnp.float32).reshape(b, S, 2, SSM_GROUPS, SSM_HEADS_PER_GROUP)
                         + dt_bias.astype(jnp.float32).reshape(2, SSM_GROUPS, SSM_HEADS_PER_GROUP))
    A = -jnp.exp(a_log.astype(jnp.float32)).reshape(2, SSM_GROUPS, SSM_HEADS_PER_GROUP)

    flip = lambda t: t[:, ::-1]
    y_fwd = ssd_chunked(xs, dt[:, :, 0], A[0], Bm, Cm)
    y_bwd = flip(ssd_chunked(flip(xs), flip(dt[:, :, 1]), A[1], flip(Bm), flip(Cm)))
    y = y_fwd + y_bwd + xs * d_skip.reshape(SSM_GROUPS, SSM_HEADS_PER_GROUP)[..., None]

    y = y.reshape(b, S, SSM_W) * jax.nn.silu(z)
    y = rms_norm(y.reshape(b, S, SSM_GROUPS, SSM_W // SSM_GROUPS),
                 norm_g.reshape(SSM_GROUPS, SSM_W // SSM_GROUPS))
    return y.reshape(b, S, SSM_W)

def setup_inputs(seed: int = 0) -> dict:
    key = jax.random.key(seed)
    ks = jax.random.split(key, 20)
    f32 = jnp.float32
    nrm = lambda k, shape, s: jax.random.normal(k, shape, f32) * s
    dt0 = jnp.exp(jax.random.uniform(ks[8], (DEPTH, 2, SSM_HEADS), f32,
                                     math.log(1e-3), math.log(1e-1)))
    return {
        "x": nrm(ks[0], (BATCH, SEQ, D_MODEL), 1.0),
        "norm_mix_g": 1.0 + nrm(ks[1], (DEPTH, D_MODEL), 0.02),
        "w_in": nrm(ks[2], (DEPTH, D_MODEL, IN_W), D_MODEL ** -0.5),
        "q_norm_g": 1.0 + nrm(ks[3], (DEPTH, ATTN_HEAD_DIM), 0.02),
        "k_norm_g": 1.0 + nrm(ks[4], (DEPTH, ATTN_HEAD_DIM), 0.02),
        "rel_bias": nrm(ks[5], (NUM_BUCKETS, ATTN_HEADS), 0.5),
        "conv_w": nrm(ks[6], (DEPTH, CONV_WIDTH, CONV_DIM), CONV_WIDTH ** -0.5),
        "conv_b": nrm(ks[7], (DEPTH, CONV_DIM), 0.01),
        "dt_bias": dt0 + jnp.log(-jnp.expm1(-dt0)),
        "a_log": jnp.log(jax.random.uniform(ks[9], (DEPTH, 2, SSM_HEADS), f32, 1.0, 16.0)),
        "d_skip": 1.0 + nrm(ks[10], (DEPTH, SSM_HEADS), 0.1),
        "ssd_norm_g": 1.0 + nrm(ks[11], (DEPTH, SSM_W), 0.02),
        "w_out": nrm(ks[12], (DEPTH, MIX_W, D_MODEL), MIX_W ** -0.5),
        "norm_mlp_g": 1.0 + nrm(ks[13], (DEPTH, D_MODEL), 0.02),
        "w_up": nrm(ks[14], (DEPTH, D_MODEL, D_FF), D_MODEL ** -0.5),
        "w_down": nrm(ks[15], (DEPTH, D_FF, D_MODEL), D_FF ** -0.5),
    }

def reference(x, norm_mix_g, w_in, q_norm_g, k_norm_g, rel_bias, conv_w, conv_b, dt_bias,
              a_log, d_skip, ssd_norm_g, w_out, norm_mlp_g, w_up, w_down):
    b, S, _ = x.shape
    splits = np.cumsum([ATTN_W, ATTN_W, ATTN_W, SSM_W, CONV_DIM]).tolist()
    for layer in range(DEPTH):
        h = rms_norm(x, norm_mix_g[layer])
        u = h @ w_in[layer]
        q, k, v, z, xbc, dt_raw = jnp.split(u, splits, axis=-1)

        heads = lambda t: t.reshape(b, S, ATTN_HEADS, ATTN_HEAD_DIM)
        q = rms_norm(heads(q), q_norm_g[layer])
        k = rms_norm(heads(k), k_norm_g[layer])
        v = heads(v)
        outs, lses = [], []
        for window, dilation in DILATED_PATTERNS:
            o, lse = dilated_window_attention(q, k, v, rel_bias, window, dilation)
            outs.append(o)
            lses.append(lse)
        wts = jax.nn.softmax(jnp.stack(lses, axis=0), axis=0)
        attn = jnp.sum(wts[..., None] * jnp.stack(outs, axis=0), axis=0)
        attn = attn.astype(x.dtype).reshape(b, S, ATTN_W)

        ssd = ssd_mixer(z, xbc, dt_raw, conv_w[layer], conv_b[layer], dt_bias[layer],
                        a_log[layer], d_skip[layer], ssd_norm_g[layer])

        x = x + jnp.concatenate([attn, ssd], axis=-1) @ w_out[layer]

        hm = rms_norm(x, norm_mlp_g[layer]) @ w_up[layer]
        x = x + jnp.square(jax.nn.relu(hm)) @ w_down[layer]
    return x


_drawn_inputs = setup_inputs


def setup_inputs(seed=0):
    import zlib

    import numpy as np

    out = dict(_drawn_inputs(seed))
    spreads = {}
    factors = {'norm_mix_g': 2.921,
     'q_norm_g': 8.0,
     'k_norm_g': 8.0,
     'conv_b': 5.512,
     'ssd_norm_g': 4.533,
     'norm_mlp_g': 3.404}
    for name, (base, spread) in spreads.items():
        noise = np.random.default_rng([zlib.crc32(name.encode()), seed]).standard_normal(out[name].shape)
        drawn = base * np.exp(spread * noise) if base else spread * noise
        out[name] = __import__('jax').numpy.asarray(drawn.astype(out[name].dtype))
    for name, factor in factors.items():
        out[name] = (out[name] * factor).astype(out[name].dtype)
    return out
```

```python
import math
from contextlib import ExitStack

import numpy as np

import concourse.bass as bass
from concourse import mybir

P = 128
SEQ, D_MODEL, D_FF = 256, 2048, 8192
HEADS, HEAD_DIM = 16, 128
SSM_HEADS, SSM_DIM, GROUPS = 32, 64, 8
PER_GROUP = SSM_HEADS // GROUPS
CONV_DIM = 4096
TAPS = 5
IN_W = 12352
BUCKETS = 32
EPS = 1e-6
PATTERNS = ((128, 1), (512, 4), (2048, 16))

TT = SEQ // P
UNIT = 512
KT = 16
CH = 8
KC = KT // CH
RING = 4
DVE_CHUNKS = (3, 7)
POOL_CHUNKS = tuple(j for j in range(CH) if j not in DVE_CHUNKS)
WIN = 3 * CH
LEAD = 3
COL_Q, COL_K, COL_V, COL_Z, COL_X = 0, 2048, 4096, 6144, 8192
COL_B, COL_C, COL_DT = 10240, 11264, 12288
GROUP_SLOT = (0, 12)
CONV_SLOTS = {0: (0, 1), 1: (2,), 6: (3,), 7: (4,)}
ROW = 384


def t5_bucket(rel):
    nb = BUCKETS // 2
    max_exact = nb // 2
    n = np.abs(rel)
    nf = np.maximum(n, 1).astype(np.float32)
    large = max_exact + (np.log(nf / np.float32(max_exact)) / np.float32(math.log(1024 / max_exact))
                         * np.float32(nb - max_exact)).astype(np.int32)
    return (rel > 0) * nb + np.where(n < max_exact, n, np.minimum(large, nb - 1))


def bias_constants():
    rel = np.arange(512) - (SEQ - 1)
    table = np.zeros((BUCKETS + 1, 512), np.float32)
    table[t5_bucket(rel), np.arange(512)] = 1.0
    count = sum(((np.abs(rel) <= window // 2) & (rel % step == 0)).astype(int) for window, step in PATTERNS)
    table[BUCKETS] = np.where(count > 0, np.log(np.maximum(count, 1)), -1e30)
    return table


def build(nc, x, norm_mix_g, w_in, q_norm_g, k_norm_g, rel_bias, conv_w, conv_b, dt_bias, a_log,
          d_skip, ssd_norm_g, w_out, norm_mlp_g, w_up, w_down, bias_table, out):
    f32, f32r = mybir.dt.float32, mybir.dt.float32r
    ALU, ACT, AX = mybir.AluOpType, mybir.ActivationFunctionType, mybir.AxisListType
    ds = bass.ds
    ctx = ExitStack()

    w_in_v = w_in[0].rearrange("(t p) n -> p t n", p=P)
    w_out_v = w_out[0].rearrange("(t p) n -> p t n", p=P)
    w_up_v = w_up[0].rearrange("(t p) n -> p t n", p=P)
    w_down_v = w_down[0].rearrange("(t p) n -> p t n", p=P)
    x_v = x[0].rearrange("(t p) (n c) -> p t n c", p=P, c=UNIT)
    out_v = out[0].rearrange("(t p) (n c) -> p t n c", p=P, c=UNIT)
    rel_rows = nc.dram_tensor("rel_rows", [HEADS, 512], f32).ap()
    rel_tiles = nc.dram_tensor("rel_tiles", [P, HEADS, ROW], f32).ap()
    decay_rows = nc.dram_tensor("decay_rows", [64, SEQ], f32).ap()

    with ctx:
        words = (nc.sbuf_usable_end - nc.sbuf_base - 64) // 32 * 8
        ctx.enter_context(nc.sbuf_tensor("arena", [P, words], f32))
        end = nc.sbuf_base
        top = [end - 4 * words]

        def place(name, shape, dt=f32, at=None):
            size = 4 * int(np.prod(shape[1:]))
            offset = top[0] if at is None else at
            if at is None:
                top[0] += (size + 31) // 32 * 32
                assert top[0] <= end, (name, top[0], end)
            return nc.alloc_sbuf_tensor_at(name, shape, dt, offset=offset)

        act_base = top[0]
        actT_hi = place("actT_hi", [P, KT, SEQ], f32r)
        actT_lo = place("actT_lo", [P, KT, SEQ], f32r)
        xres = place("xres", [P, 4, TT, UNIT], f32, at=act_base)
        cat_base = top[0]
        cat_hi = place("cat_hi", [P, 2 * KT, SEQ], f32r)
        cat_lo = place("cat_lo", [P, 2 * KT, SEQ], f32r)
        hid_hi = place("hid_hi", [P, KT, SEQ], f32r, at=cat_base)
        hid_lo = place("hid_lo", [P, KT, SEQ], f32r, at=cat_base + KT * SEQ * 4)
        raw = [place(f"raw{j}", [P, KC, UNIT]) for j in range(CH)]
        w_hi = [place(f"w_hi{j}", [P, KC, UNIT], f32r) for j in range(RING)]
        w_lo = [place(f"w_lo{j}", [P, KC, UNIT], f32r) for j in range(RING)]
        ident = place("ident", [P, P])
        ones = place("ones", [P, P])
        parA = place("parA", [P, P])
        parB = place("parB", [P, 114])
        gqk = place("gqk", [P, 1])
        small = place("small", [P, 48])
        halfneg = place("halfneg", [P, 8])
        dskip = place("dskip", [P, 16])
        dskip_all = place("dskip_all", [P, SSM_HEADS])
        tokp = place("tokp", [P, 5, 64])
        phase = top[0]

        x_in = place("x_in", [P, TT, D_MODEL], at=cat_base)
        junk = place("junk", [P, D_MODEL], at=cat_base + 16384)
        rowsA = place("rowsA", [P, P], at=cat_base + 24576)
        rowsB = place("rowsB", [114, P], at=cat_base + 25088)
        relw = place("relw", [BUCKETS + 1, HEADS], at=cat_base + 25600)
        reltab = place("reltab", [BUCKETS + 1, 512], at=cat_base + 25664)
        relout = place("relout", [HEADS, 512], at=cat_base + 27712)
        junk2 = place("junk2", [P, D_MODEL], at=phase + 16384)
        xg = [place(f"xg{i}", [P, KC, SEQ], at=phase + 2048 * i) for i in range(2)]

        ssd = [cat_base, cat_base + 16384, cat_base + 32768, cat_base + 32768 + 16384]

        def at_of(cursor, size):
            offset = cursor[0]
            cursor[0] += size
            return offset

        lo1 = [cat_base + 32768]
        dt_raw = place("dt_raw", [P, KT, 64], at=at_of(lo1, 4096))
        dt_hi = place("dt_hi", [P, KT, 64], f32r, at=at_of(lo1, 4096))
        dt_lo = place("dt_lo", [P, KT, 64], f32r, at=at_of(lo1, 4096))
        lo2 = [cat_base + 32768]
        gate_t = place("gate_t", [P, 2, SEQ], at=at_of(lo2, 2048))
        gate = place("gate", [P, 2, SEQ], at=at_of(lo2, 2048))
        gate_sq = place("gate_sq", [P, 2, SEQ], at=at_of(lo2, 2048))
        xtok = place("xtok", [P, TT, SEQ], at=at_of(lo2, 2048))
        mean_sq = place("mean_sq", [P, SEQ], at=at_of(lo2, 1024))
        log_ms = place("log_ms", [P, SEQ], at=at_of(lo2, 1024))
        rnorm = place("rnorm", [P, SEQ], at=at_of(lo2, 1024))
        newton = place("newton", [P, SEQ], at=at_of(lo2, 1024))
        gate_n = gate_t
        hi1 = [phase + 4096]
        mask = place("mask", [P, 6, P], at=at_of(hi1, 3072))
        cbm = place("cbm", [P, 6, P], at=at_of(hi1, 3072))
        mix = [place(f"mix{i}", [P, 6, P], at=at_of(hi1, 3072)) for i in range(PER_GROUP)]
        decay = place("decay", [P, 2, PER_GROUP, SEQ], at=at_of(hi1, 8192))
        zs = place("zs", [P, 4, SEQ], at=at_of(hi1, 4096))
        conv_in = place("conv_in", [P, 2, 4, SEQ + 4], at=at_of(hi1, 8320))
        assert hi1[0] <= end, (hi1[0], end)
        lo3 = [cat_base]
        conv = place("conv", [P, 4, SEQ], at=at_of(lo3, 4096))
        conv_t = place("conv_t", [P, 4, SEQ], at=at_of(lo3, 4096))
        xbc = place("xbc", [P, 4, SEQ], at=at_of(lo3, 4096))
        lo4 = [cat_base + 32768 + 16384]
        dtv = {n: place("dt_" + n, [64, SEQ], at=at_of(lo4, 1024))
               for n in ("v", "e", "r", "z", "z2", "p", "soft", "a")}
        prefix = place("prefix", [64, TT, P + 1], at=at_of(lo4, 1088))
        dt_rows = place("dt_rows", [64, 5, P], at=at_of(lo4, 2560))
        dtcol = place("dtcol", [64, 8], at=at_of(lo4, 64))
        one_row = place("one_row", [64, P], at=at_of(lo4, 512))

        qk_n = [place(n, [P, TT, UNIT], at=cat_base + 32768 * i + 12288) for i, n in enumerate(("q_n", "k_n"))]
        att = [phase]
        sq_tmp = place("sq_tmp", [P, TT, UNIT], at=at_of(att, 4096))
        v_tok = place("v_tok", [P, TT, UNIT], at=at_of(att, 4096))
        qkT = place("qkT", [P, 4, 2, SEQ], at=at_of(att, 8192))
        bias_t = [place(f"bias_t{i}", [P, ROW], at=at_of(att, 4 * ROW)) for i in range(2)]
        prob = [place(f"prob{i}", [P, TT, SEQ], at=at_of(att, 2048)) for i in range(2)]
        probT = place("probT", [P, TT, SEQ], at=at_of(att, 2048))
        soft = place("soft", [P, 2, 4, TT], at=at_of(att, 64))
        qk_s = small[:, 8:32].rearrange("p (a h) -> p a h", a=3)
        assert att[0] <= end
        mlp = [phase + 4096]
        acc = place("acc", [P, 4, TT, UNIT], at=at_of(mlp, 16384))
        sq_junk = place("sq_junk", [P, UNIT], at=at_of(mlp, 2048))
        relu_t = place("relu_t", [P, 4, SEQ], at=at_of(mlp, 4096))
        relu_sq = place("relu_sq", [P, 4, SEQ], at=at_of(mlp, 4096))
        ssum = place("ssum", [P, TT, 4], at=at_of(mlp, 32))
        inv_ms = place("inv_ms", [P, 3, TT], at=at_of(mlp, 32))
        assert mlp[0] <= end

        psum = ctx.enter_context(nc.psum_tensor("psum", [P, 8, UNIT], f32))
        M0, M1 = psum[:, 6, :], psum[:, 7, :]

        def bank_pair(n):
            return psum[:, 2 * n:2 * n + 2, :]

        def tiles(n):
            return bank_pair(n).rearrange("p b (t s) -> p (b t) s", t=2)

        def sem(name):
            return ctx.enter_context(nc.semaphore(name))

        raw_in = [sem(f"raw_in{j}") for j in range(CH)]
        hi_ready, lo_pool, lo_dve, chunk_used = sem("hi_ready"), sem("lo_pool"), sem("lo_dve"), sem("chunk_used")
        x_in_s = [sem(f"x_in{t}") for t in range(TT)]
        rows_in, relw_in, col_in, dtw_in, dskip_in = (sem(n) for n in (
            "rows_in", "relw_in", "col_in", "dtw_in", "dskip_in"))
        consts, pool_masks = sem("consts"), sem("pool_masks")
        x_sq, x_sq_dve, x_ms, x_rs, x_scaled, x_scaled_act = (sem(n) for n in (
            "x_sq", "x_sq_dve", "x_ms", "x_rs", "x_scaled", "x_scaled_act"))
        params_t, params_ready, rel_done, rel_copied, rel_stored = (sem(n) for n in (
            "params_t", "params_ready", "rel_done", "rel_copied", "rel_stored"))
        xt_done, xg_ready, xh_ready, xl_ready = (sem(n) for n in ("xt_done", "xg_ready", "xh_ready", "xl_ready"))
        dt_hi_ready, dt_lo_ready, dt_done, dt_act, dt_step, dt_tok, decay_stored = (sem(n) for n in (
            "dt_hi_ready", "dt_lo_ready", "dt_done", "dt_act", "dt_step", "dt_tok", "decay_stored"))
        m0_free, m1_free = sem("m0_free"), sem("m1_free")
        xbc_in, conv_step, conv_tanh, xbc_ready = (sem(n) for n in (
            "xbc_in", "conv_step", "conv_tanh", "xbc_ready"))
        decay_in = sem("decay_in")
        args_ready, decays_ready, scaled, mix_ready, y_done = (sem(n) for n in (
            "args_ready", "decays_ready", "scaled", "mix_ready", "y_done"))
        x_transposed, xtok_ready, cb_done, cb_masked = (sem(n) for n in (
            "x_transposed", "xtok_ready", "cb_done", "cb_masked"))
        gated, gate_squared, norm_summed, ln_ready, rn_ready, newton_step, normed, ssd_hi, ssd_lo = (sem(n) for n in (
            "gated", "gate_squared", "norm_summed", "ln_ready", "rn_ready", "newton_step", "normed", "ssd_hi", "ssd_lo"))
        z_tanh, z_ready = sem("z_tanh"), sem("z_ready")
        qk_sq, qk_ss, qk_ms, qk_rs, qk_normed, v_copied = (sem(n) for n in (
            "qk_sq", "qk_ss", "qk_ms", "qk_rs", "qk_normed", "v_copied"))
        bias_in = [sem(f"bias_in{i}") for i in range(2)]
        qk_transposed, qkT_ready, scores, logits, neg_max, probs, recip, p_normed = (sem(n) for n in (
            "qk_transposed", "qkT_ready", "scores", "logits", "neg_max", "probs", "recip", "p_normed"))
        p_transposed, pT_ready, pv_done, att_hi, att_lo = (sem(n) for n in (
            "p_transposed", "pT_ready", "pv_done", "att_hi", "att_lo"))
        xres_in, added, squared_mid, mid_step = sem("xres_in"), sem("added"), sem("squared_mid"), sem("mid_step")
        relu_done, relu_squared, hid_hi_s, hid_lo_s, down_added, out_stored = (sem(n) for n in (
            "relu_done", "relu_squared", "hid_hi_s", "hid_lo_s", "down_added", "out_stored"))

        block = ctx.enter_context(nc.Block())

        def positive(count):
            return not isinstance(count, int) or count > 0

        def wait_low(eng, U, j):
            if j in DVE_CHUNKS:
                eng.wait_ge(lo_dve, len(DVE_CHUNKS) * U + DVE_CHUNKS.index(j) + 1)
            else:
                eng.wait_ge(lo_pool, len(POOL_CHUNKS) * U + POOL_CHUNKS.index(j) + 1)

        MIX_UNITS = 24
        OUT_U = MIX_UNITS
        MLP_U = OUT_U + 8

        @block.sync
        def _(sp):
            def load(U, j, pieces):
                if positive(U):
                    wait_low(sp, U - 1, j)
                at = 0
                for src in pieces:
                    n = src.shape[-1]
                    sp.dma_start(raw[j][:, :, at:at + n], src).then_inc(raw_in[j], 16 * len_of[len(pieces)])
                    at += n

            len_of = {1: 3, 3: 1}

            def in_cols(j, c0, n=UNIT):
                return w_in_v[:, KC * j:KC * (j + 1), ds(c0, n)]

            def ssd_window(w, m):
                for s in range(WIN):
                    r, j = divmod(s, CH)
                    if r < 2:
                        g = 2 * w + r
                        load(3 * w + r, j, [in_cols(j, COL_X + 256 * g, 256), in_cols(j, COL_B + 128 * g, 128),
                                            in_cols(j, COL_C + 128 * g, 128)])
                    else:
                        load(3 * w + r, j, [in_cols(j, COL_Z + UNIT * w)])
                    decay_loads(s, w, m)

            def load_decay(g):
                src = decay_rows.rearrange("(d h) s -> d h s", d=2)[:, ds(PER_GROUP * g, PER_GROUP), :]
                for d in range(2):
                    sp.dma_start(decay[:, d], src[d:d + 1].broadcast_to([P, PER_GROUP, SEQ])).then_inc(decay_in, 16)

            def decay_loads(s, w, m):
                if s == 13 and m is not None:
                    sp.wait_ge(args_ready, 8 * m + 4)
                    load_decay(2 * m + 1)
                if s == 23 and w is not None:
                    if positive(w):
                        sp.wait_ge(args_ready, 8 * w)
                    else:
                        sp.wait_ge(decay_stored, 32)
                    load_decay(2 * w)

            def load_bias(s, g):
                if s in (10, 14, 18, 22):
                    h = (s - 10) // 4
                    sp.wait_ge(logits, 4 * g + h + 1)
                    sp.dma_start(bias_t[h % 2][:, :].rearrange("p (o j) -> p o j", o=1),
                                 rel_tiles[:, ds(4 * g + h, 1), :]).then_inc(bias_in[h % 2], 16)

            def att_window(a, m, g):
                for s in range(WIN):
                    r, j = divmod(s, CH)
                    load(12 + 3 * a + r, j, [in_cols(j, (COL_Q, COL_K, COL_V)[r] + UNIT * a)])
                    if m is not None:
                        decay_loads(s, None, m)
                    if g is not None:
                        load_bias(s, g)

            sp.dma_start(x_in[:, 0, :].rearrange("p (n c) -> p n c", c=UNIT), x_v[:, 0]).then_inc(x_in_s[0], 16)
            ssd_window(0, None)
            with sp.Fori(1, 4) as w:
                ssd_window(w, w - 1)
            sp.wait_ge(rel_stored, 32)
            att_window(0, 3, None)
            with sp.Fori(1, 4) as a:
                att_window(a, None, a - 1)
            for n in range(8):
                slab = 1 - n // 4
                for j in range(CH):
                    s = CH * n + j
                    load(OUT_U + n, j, [w_out_v[:, KT * slab + KC * j:KT * slab + KC * (j + 1),
                                                UNIT * (n % 4):UNIT * (n % 4 + 1)]])
                    load_bias(s, 3)
                    if s == 12:
                        sp.wait_ge(chunk_used, CH * MIX_UNITS)
                        for t in range(TT):
                            sp.dma_start(xres[:, :, t, :], x_v[:, t]).then_inc(xres_in, 16)

            def mlp_quarter(q):
                for n in range(4):
                    for j in range(CH):
                        load(MLP_U + 8 * q + n, j, [w_up_v[:, KC * j:KC * (j + 1), ds(2048 * q + UNIT * n, UNIT)]])
                for n in range(4):
                    for j in range(CH):
                        load(MLP_U + 8 * q + 4 + n, j, [w_down_v[:, ds(KT * q + KC * j, KC), UNIT * n:UNIT * (n + 1)]])

            mlp_quarter(0)
            with sp.Fori(1, 4) as q:
                mlp_quarter(q)
            for n in range(4):
                sp.wait_ge(down_added, 4 * 3 + n + 1)
                for t in range(TT):
                    sp.dma_start(out_v[:, t, n, :], acc[:, n, t, :]).then_inc(out_stored, 16)
            sp.wait_ge(out_stored, 16 * 4 * TT)

        @block.gpsimd
        def _(pool):
            pool.memset(ident[:, :], 1.0).then_inc(consts, 1)
            pool.memset(ones[:, :], 1.0).then_inc(consts, 1)
            pool.memset(halfneg[:, :], -0.5).then_inc(consts, 1)
            pool.memset(relw[:, :], 1.0).then_inc(consts, 1)
            pool.memset(one_row[:, :], 1.0).then_inc(consts, 1)
            pool.memset(prefix[:, :, 0:1], 0.0).then_inc(consts, 1)
            pool.memset(conv_in[:, :, :, 0:2], 0.0).then_inc(consts, 1)
            pool.memset(conv_in[:, :, :, SEQ + 2:SEQ + 4], 0.0).then_inc(consts, 1)
            pool.memset(dtcol[:, 3:4], 1.0).then_inc(consts, 1)
            pool.memset(mask[:, :, :], 1.0).then_inc(consts, 1)
            pool.wait_ge(consts, 10)
            pool.memset(dtcol[0:32, 3:4], -1.0).then_inc(consts, 1)
            pool.wait_ge(consts, 11)
            pool.affine_select(out=ident[:, :], in_=ident[:, :], compare_op=ALU.is_equal, fill=0.0, base=0,
                               pattern=[[-1, P]], channel_multiplier=1).then_inc(pool_masks, 1)
            for i in (0, 2):
                pool.affine_select(out=mask[:, i, :], in_=mask[:, i, :], compare_op=ALU.is_ge, fill=0.0, base=0,
                                   pattern=[[1, P]], channel_multiplier=-1).then_inc(pool_masks, 1)
            for i in (3, 5):
                pool.affine_select(out=mask[:, i, :], in_=mask[:, i, :], compare_op=ALU.is_ge, fill=0.0, base=0,
                                   pattern=[[-1, P]], channel_multiplier=1).then_inc(pool_masks, 1)
            pool.wait_ge(x_ms, 1)
            pool.tensor_tensor(small[:, 4:6], small[:, 2:4], halfneg[:, 0:2], ALU.pow).then_inc(x_rs, 1)

            def low(U, j):
                i = j % RING
                pool.wait_ge(hi_ready, CH * U + j + 1)
                pool.tensor_tensor(w_lo[i][:, :, :], raw[j][:, :, :], w_hi[i][:, :, :].bitcast(f32),
                                   ALU.subtract).then_inc(lo_pool, 1)

            def unit(U):
                for j in POOL_CHUNKS:
                    low(U, j)

            def qk_root(n):
                pool.wait_ge(qk_ms, n + 1)
                pool.tensor_tensor(qk_s[:, 2, :], qk_s[:, 1, :], halfneg[:, :], ALU.pow).then_inc(qk_rs, 1)

            def att_window(a):
                for s in range(WIN):
                    r, j = divmod(s, CH)
                    if j in POOL_CHUNKS:
                        low(12 + 3 * a + r, j)
                    if s == 11 + LEAD:
                        qk_root(2 * a)
                    if s == 19 + LEAD:
                        qk_root(2 * a + 1)

            for U in range(3):
                unit(U)
            with pool.Fori(3, 12) as U:
                unit(U)
            att_window(0)
            with pool.Fori(1, 4) as a:
                att_window(a)
            with pool.Fori(OUT_U, MLP_U + 32) as U:
                unit(U)

        @block.scalar
        def _(act):
            act.dma_start(x_in[:, 1, :].rearrange("p (n c) -> p n c", c=UNIT), x_v[:, 1]).then_inc(x_in_s[1], 16)
            act.dma_start(rowsA[:, :], conv_w[0, 0:4, :].rearrange("k (t p) -> (k t) p", p=P)).then_inc(rows_in, 16)
            act.dma_start(rowsB[0:32, :], conv_w[0, 4, :].rearrange("(t p) -> t p", p=P)).then_inc(rows_in, 16)
            act.dma_start(rowsB[32:64, :], conv_b[0].rearrange("(t p) -> t p", p=P)).then_inc(rows_in, 16)
            act.dma_start(rowsB[64:80, :], norm_mix_g[0].rearrange("(t p) -> t p", p=P)).then_inc(rows_in, 16)
            act.dma_start(rowsB[80:96, :], norm_mlp_g[0].rearrange("(t p) -> t p", p=P)).then_inc(rows_in, 16)
            act.dma_start(rowsB[96:112, :], ssd_norm_g[0].rearrange("(t p) -> t p", p=P)).then_inc(rows_in, 16)
            act.dma_start(rowsB[112:113, :], q_norm_g[0:1, :]).then_inc(rows_in, 16)
            act.dma_start(rowsB[113:114, :], k_norm_g[0:1, :]).then_inc(rows_in, 16)
            act.dma_start(dt_raw[:, :, :], w_in_v[:, :, COL_DT:COL_DT + 64]).then_inc(dtw_in, 16)
            act.dma_start(reltab[:, :], bias_table).then_inc(relw_in, 16)
            act.dma_start(dtcol[:, 0:1], dt_bias[0].rearrange("d (h o) -> (d h) o", o=1)).then_inc(col_in, 16)
            act.dma_start(dtcol[:, 1:2], a_log[0].rearrange("d (h o) -> (d h) o", o=1)).then_inc(col_in, 16)
            act.dma_start(dskip_all[:, :], d_skip[0:1, :].broadcast_to([P, SSM_HEADS])).then_inc(dskip_in, 16)
            act.wait_ge(consts, 4)
            act.dma_start(relw[0:BUCKETS, :], rel_bias).then_inc(relw_in, 16)

            act.wait_ge(x_in_s[0], 16)
            act.activation(junk[:, :], x_in[:, 0, :], ACT.Square, accum_out=small[:, 0:1]).then_inc(x_sq, 1)
            act.wait_ge(x_rs, 1)
            act.activation(x_in[:, 0, :], x_in[:, 0, :], ACT.Copy, scale=small[:, 4:5]).then_inc(x_scaled_act, 1)

            def x_high(R):
                r = R % 8
                act.wait_ge(xg_ready, R + 1)
                act.activation(actT_hi[:, KC * r:KC * r + KC, :], xg[R % 2][:, :, :], ACT.Copy).then_inc(xh_ready, 1)

            def high(U, j):
                act.wait_ge(raw_in[j], 48 * (U + 1))
                if positive(CH * U + j - RING + 1):
                    act.wait_ge(chunk_used, CH * U + j - RING + 1)
                act.activation(w_hi[j % RING][:, :, :], raw[j][:, :, :], ACT.Copy).then_inc(hi_ready, 1)

            def high_ahead(U0, s):
                n, j = divmod(s + LEAD, CH)
                high(U0 + n, j)

            def xbc_copy(G, i):
                act.wait_ge(chunk_used, 24 * G_pair(G, i) + CH * (i + 1))
                if not isinstance(G, int) or G > 1:
                    act.wait_ge(conv_step, 20 * (G - 1))
                act.wait_ge(consts, 8)
                act.activation(conv_in[:, i, :, 2:2 + SEQ], tiles(i), ACT.Copy).then_inc(xbc_in, 1)

            def G_pair(G, i):
                return (G - i) // 2 if isinstance(G, int) else pair_of[0]

            pair_of = [None]

            def z_tanh_of(m):
                act.wait_ge(chunk_used, 24 * (m + 1))
                act.wait_ge(gated, 2 * m + 1)
                act.activation(zs[:, :, :], tiles(2), ACT.Tanh, scale=0.5).then_inc(z_tanh, 1)

            def head_exp(H, h):
                act.wait_ge(args_ready, H + 1)
                act.activation(mix[h][:, :, :], mix[h][:, :, :], ACT.Exp).then_inc(decays_ready, 1)

            def conv_tanh_of(G):
                act.wait_ge(conv_step, 20 * (G + 1))
                act.activation(conv_t[:, :, :], conv[:, :, :], ACT.Tanh).then_inc(conv_tanh, 1)

            def ssd_slot(s, m, more=True):
                for i, o in enumerate(GROUP_SLOT):
                    G, k = 2 * m + i, s - o
                    if k in (0, 1):
                        for h in (2 * k, 2 * k + 1):
                            head_exp(4 * G + h, h)
                    if k == 2:
                        act.wait_ge(x_transposed, G + 1)
                        act.activation(xtok[:, :, :], M0.rearrange("p (t s) -> p t s", t=2), ACT.Copy)\
                            .then_inc(xtok_ready, 1)
                    if k == 8:
                        act.wait_ge(gated, G + 2)
                        act.activation(gate_sq[:, :, :], gate[:, :, :], ACT.Square).then_inc(gate_squared, 1)
                    if k == 8 and (i == 0 or more):
                        conv_tanh_of(G + 1)
                    if k == 10:
                        act.wait_ge(m1_free, G + 2)
                        act.activation(log_ms[:, :], mean_sq[:, :], ACT.Ln).then_inc(ln_ready, 1)
                        act.wait_ge(ln_ready, G + 1)
                        act.activation(rnorm[:, :], log_ms[:, :], ACT.Exp, scale=-0.5).then_inc(rn_ready, 1)
                    if k == 11:
                        act.wait_ge(normed, G + 1)
                        for c in range(2):
                            ins = act.activation(cat_hi[:, ds(KT + 2 * G + c, 1), :], gate_n[:, c:c + 1, :], ACT.Copy,
                                                 scale=parB[:, ds(96 + 2 * G + c, 1)])
                        ins.then_inc(ssd_hi, 1)

            def qk_square(n, a):
                i = n_parity[0]
                act.wait_ge(chunk_used, 24 * (4 + a) + CH * (i + 1))
                if positive(n):
                    act.wait_ge(qk_ss, n)
                act.activation(sq_tmp[:, :, :], bank_pair(i), ACT.Square).then_inc(qk_sq, 1)

            n_parity = [0]

            def v_copy(a):
                act.wait_ge(chunk_used, 24 * (5 + a))
                act.wait_ge(att_lo, 4 * a + 1)
                act.activation(v_tok[:, :, :], bank_pair(2), ACT.Copy).then_inc(v_copied, 1)

            def att_slot(s, g):
                for h in range(4):
                    H = 4 * g + h
                    if s == 6 + 4 * h:
                        act.wait_ge(neg_max, H + 1)
                        for t in range(TT):
                            ins = act.activation(prob[h % 2][:, t, :], prob[h % 2][:, t, :], ACT.Exp,
                                                 bias=soft[:, h % 2, 1, t:t + 1], accum_out=soft[:, h % 2, 2, t:t + 1])
                        ins.then_inc(probs, 1)
                    if s == 8 + 4 * h:
                        act.wait_ge(p_transposed, H + 1)
                        act.activation(probT[:, :, :], M1.rearrange("p (t s) -> p t s", t=2), ACT.Copy)\
                            .then_inc(pT_ready, 1)
                    if s == 10 + 4 * h:
                        act.wait_ge(pv_done, H + 1)
                        act.activation(cat_hi[:, ds(H, 1), :], M1[:, 0:SEQ].rearrange("p (o s) -> p o s", o=1),
                                       ACT.Copy).then_inc(att_hi, 1)

            for R in range(8):
                if R >= RING:
                    high(0, R)
                x_high(R)
                if R < RING:
                    high(0, R)
            act.wait_ge(dtw_in, 16)
            act.activation(dt_hi[:, :, :], dt_raw[:, :, :], ACT.Copy).then_inc(dt_hi_ready, 1)
            act.wait_ge(col_in, 32)
            act.activation(dtcol[:, 2:3], dtcol[:, 1:2], ACT.Exp).then_inc(dt_act, 1)
            for s in range(CH - LEAD, WIN):
                high_ahead(0, s)
                if s == 5:
                    act.wait_ge(rel_copied, 1)
                    act.dma_start(rel_rows, relout[:, :]).then_inc(rel_stored, 16)
                if s == 7:
                    act.wait_ge(dt_step, 2)
                    act.activation(dtv["e"][:, :], dtv["e"][:, :], ACT.Exp, scale=-1.0).then_inc(dt_act, 1)
                if s == 8:
                    act.wait_ge(rel_stored, 16)
                    act.dma_start(rel_tiles.rearrange("p h j -> h p j"),
                                  bass.AP(rel_rows.tensor, P - 1, [[512, HEADS], [-1, P], [1, ROW]]))\
                        .then_inc(rel_stored, 16)
                if s == 11:
                    act.wait_ge(dt_step, 20)
                    act.dma_start(decay_rows[0:32, :].rearrange("h (c s) -> h c s", c=TT),
                                  prefix[0:32, :, 1:P + 1]).then_inc(decay_stored, 16)
                    act.dma_start(decay_rows[32:64, :].rearrange("h (c s) -> h c s", c=TT),
                                  prefix[32:64, :, 0:P]).then_inc(decay_stored, 16)
                if s == 10:
                    xbc_copy(0, 0)
                if s == 18:
                    xbc_copy(1, 1)
                if s == GROUP_SLOT[1] + 8:
                    conv_tanh_of(0)

            def ssd_window(w, m):
                for s in range(WIN):
                    high_ahead(3 * w, s)
                    if s == 2:
                        z_tanh_of(m)
                    ssd_slot(s, m)
                    if s == 10:
                        pair_of[0] = w
                        xbc_copy(2 * w, 0)
                    if s == 18:
                        pair_of[0] = w
                        xbc_copy(2 * w + 1, 1)

            def att_window(a, m, g):
                for s in range(WIN):
                    high_ahead(12 + 3 * a, s)
                    if m is not None:
                        if s == 2:
                            z_tanh_of(m)
                        ssd_slot(s, m, False)
                    if g is not None:
                        if s == 2:
                            v_copy(g)
                        att_slot(s, g)
                    if s == 10:
                        n_parity[0] = 0
                        qk_square(2 * a, a)
                    if s == 18:
                        n_parity[0] = 1
                        qk_square(2 * a + 1, a)

            with act.Fori(1, 4) as w:
                ssd_window(w, w - 1)
            att_window(0, 3, None)
            with act.Fori(1, 4) as a:
                att_window(a, None, a - 1)
            for n in range(8):
                for j in range(CH):
                    s = CH * n + j
                    high_ahead(OUT_U, s)
                    if s == 2:
                        v_copy(3)
                    att_slot(s, 3)
                    if n > 4 and j == 4:
                        mid_block_act = n - 5
                        for t in range(TT):
                            act.wait_ge(added, 4 + mid_block_act + 1)
                            if positive(TT * mid_block_act + t):
                                act.wait_ge(squared_mid, TT * mid_block_act + t)
                            act.activation(sq_junk[:, :], acc[:, mid_block_act, t, :], ACT.Square,
                                           accum_out=ssum[:, t, mid_block_act:mid_block_act + 1]).then_inc(squared_mid, 1)
                        x_high(8 + 2 * mid_block_act)
                        x_high(9 + 2 * mid_block_act)
            x_high(14)
            x_high(15)
            for t in range(TT):
                act.wait_ge(added, 8)
                act.wait_ge(squared_mid, TT * 3 + t)
                act.activation(sq_junk[:, :], acc[:, 3, t, :], ACT.Square,
                               accum_out=ssum[:, t, 3:4]).then_inc(squared_mid, 1)

            def relu(U, n, q):
                act.wait_ge(chunk_used, CH * (U + 1))
                if positive(4 * q + n):
                    act.wait_ge(relu_squared, 4 * q + n)
                act.activation(relu_t[:, :, :], tiles(n), ACT.Relu).then_inc(relu_done, 1)

            def hid_high(n, q):
                act.wait_ge(relu_squared, 4 * q + n + 1)
                act.activation(hid_hi[:, 4 * n:4 * n + 4, :], relu_sq[:, :, :], ACT.Copy).then_inc(hid_hi_s, 1)

            def mlp_quarter(q, start):
                for s in range(start, 8 * CH):
                    n, j = divmod(s, CH)
                    high(MLP_U + 8 * q + n, j)
                    if 1 <= n <= 4 and j == 2:
                        relu(MLP_U + 8 * q + n - 1, n - 1, q)
                    if 1 <= n <= 4 and j == 3:
                        hid_high(n - 1, q)

            mlp_quarter(0, LEAD)
            with act.Fori(1, 4) as q:
                mlp_quarter(q, 0)

        @block.vector
        def _(dve):
            tt_, ts_, stt_ = dve.tensor_tensor, dve.tensor_scalar, dve.scalar_tensor_tensor
            dve.sem_inc(gated, 1)
            dve.sem_inc(att_lo, 1)
            dve.sem_inc(logits, 2)

            dve.wait_ge(x_in_s[1], 16)
            dve.tensor_tensor_reduce(out=junk2[:, :], in0=x_in[:, 1, :], in1=x_in[:, 1, :], scale=1.0, scalar=0.0,
                                     op0=ALU.mult, op1=ALU.add, accum_out=small[:, 1:2]).then_inc(x_sq_dve, 1)
            dve.wait_ge(x_sq_dve, 1)
            dve.wait_ge(x_sq, 1)
            ts_(small[:, 2:4], small[:, 0:2], 1.0 / D_MODEL, EPS, ALU.mult, ALU.add).then_inc(x_ms, 1)
            dve.wait_ge(x_rs, 1)
            ts_(x_in[:, 1, :], x_in[:, 1, :], small[:, 5:6], None, ALU.mult).then_inc(x_scaled, 1)

            dve.wait_ge(params_t, 1)
            dve.tensor_copy(parA[:, :], M0[:, 0:P]).then_inc(params_ready, 1)
            dve.tensor_copy(parB[:, :], M0[:, P:P + 114]).then_inc(params_ready, 1)
            dve.wait_ge(params_ready, 2)
            ts_(parA[:, :], parA[:, :], 0.5, None, ALU.mult).then_inc(params_ready, 1)
            ts_(parB[:, 0:64], parB[:, 0:64], 0.5, None, ALU.mult).then_inc(params_ready, 1)
            ts_(parB[:, 96:112], parB[:, 96:112], 0.5, None, ALU.mult).then_inc(params_ready, 1)
            ts_(gqk[:, :], parB[:, 112:113], parB[:, 113:114], 1.0 / math.sqrt(HEAD_DIM), ALU.mult, ALU.mult)\
                .then_inc(params_ready, 1)
            dve.wait_ge(dskip_in, 16)
            for i in range(2):
                dve.tensor_copy(dskip[64 * i:64 * i + 64, :], dskip_all[64 * i:64 * i + 64, i:SSM_HEADS:2])\
                    .then_inc(params_ready, 1)
            def x_gain(R, g0):
                r = R % 8
                dve.wait_ge(xt_done, R + 1)
                if positive(R - 1):
                    dve.wait_ge(xh_ready, R - 1)
                if positive(R - 1):
                    dve.wait_ge(xl_ready, R - 1)
                gain = parB[:, g0 + KC * r:g0 + KC * r + KC].rearrange("p (t o) -> p t o", o=1)\
                    .broadcast_to([P, KC, SEQ])
                tt_(xg[R % 2][:, :, :], (M0, M1)[R % 2].rearrange("p (t s) -> p t s", t=KC), gain, ALU.mult)\
                    .then_inc(xg_ready, 1)

            def x_low(R):
                r = R % 8
                dve.wait_ge(xh_ready, R + 1)
                tt_(actT_lo[:, KC * r:KC * r + KC, :], xg[R % 2][:, :, :],
                    actT_hi[:, KC * r:KC * r + KC, :].bitcast(f32), ALU.subtract).then_inc(xl_ready, 1)

            def low(U, j):
                i = j % RING
                dve.wait_ge(hi_ready, CH * U + j + 1)
                tt_(w_lo[i][:, :, :], raw[j][:, :, :], w_hi[i][:, :, :].bitcast(f32), ALU.subtract).then_inc(lo_dve, 1)

            def low_ahead(U0, s):
                n, j = divmod(s + LEAD, CH)
                if j in DVE_CHUNKS:
                    low(U0 + n, j)

            def decay_args(G, h):
                H, w, rows = 4 * G + h, mix[h], decay
                dve.wait_ge(decay_in, 32 * (G + 1))
                dve.wait_ge(y_done, H + 1)
                f, b = ds(H, 1), ds(32 + H, 1)
                for k, (d, l, src, col) in enumerate((
                        (0, 0, 0, f), (0, 1, 2, f), (0, 1, 1, f), (1, 0, 0, b), (1, 0, 2, b), (1, 1, 1, b))):
                    ins = ts_(w[:, k, :], rows[:, d, h, P * l:P * l + P], tokp[:, src, col], 0.0, ALU.add, ALU.min)
                ins.then_inc(args_ready, 1)

            def mix_head(G, h):
                H, w = 4 * G + h, mix[h]
                dve.wait_ge(decays_ready, H + 1)
                dve.wait_ge(cb_masked, G + 1)
                for k0, k1, src, col in ((0, 2, 3, H), (2, 3, 4, H), (3, 4, 3, 32 + H), (4, 6, 4, 32 + H)):
                    ins = stt_(w[:, k0:k1, :], w[:, k0:k1, :], tokp[:, src, ds(col, 1)], cbm[:, k0:k1, :],
                               ALU.mult, ALU.mult)
                ins.then_inc(scaled, 1)
                dve.wait_ge(scaled, H + 1)
                tt_(w[:, 0:6:5, :], w[:, 0:3:2, :], w[:, 3:6:2, :], ALU.add).then_inc(mix_ready, 1)

            def convolve(G, i, taps):
                dve.wait_ge(xbc_in, G + 1)
                if 0 in taps and positive(G):
                    dve.wait_ge(xbc_ready, G)
                for k in taps:
                    for c in range(4):
                        tile = 2 * G + c if c < 2 else (16 + G if c == 2 else 24 + G)
                        wt = parA[:, ds(32 * k + tile, 1)] if k < 4 else parB[:, ds(tile, 1)]
                        src = conv_in[:, i, c, k:k + SEQ]
                        if k == 0:
                            ts_(conv[:, c, :], src, wt, parB[:, ds(32 + tile, 1)], ALU.mult, ALU.add)\
                                .then_inc(conv_step, 1)
                        else:
                            dve.wait_ge(conv_step, 20 * G + 4 * (k - 1) + c + 1)
                            stt_(conv[:, c, :], src, wt, conv[:, c, :], ALU.mult, ALU.add).then_inc(conv_step, 1)

            def silu(G):
                dve.wait_ge(conv_tanh, G + 1)
                stt_(xbc[:, :, :], conv_t[:, :, :], 1.0, conv[:, :, :], ALU.add, ALU.mult).then_inc(xbc_ready, 1)

            def mask_cb(G):
                dve.wait_ge(cb_done, G + 1)
                cb = M1.rearrange("p (t l) -> p t l", l=P)
                for k0, k1, b in ((0, 2, 0), (2, 3, 3), (3, 4, 0), (4, 6, 2)):
                    ins = tt_(cbm[:, k0:k1, :], cb[:, b:b + k1 - k0, :], mask[:, k0:k1, :], ALU.mult)
                ins.then_inc(cb_masked, 1)

            def gate_group(G, i):
                dve.wait_ge(y_done, 4 * G + 8)
                for c in range(2):
                    ins = stt_(gate_t[:, c, :], xbc[:, c, :], dskip[:, ds(2 * G + c, 1)],
                               M0[:, SEQ * c:SEQ * (c + 1)], ALU.mult, ALU.add)
                ins.then_inc(m0_free, 1)
                dve.wait_ge(m0_free, G + 2)
                dve.wait_ge(z_ready, pair_of[0] + 1)
                tt_(gate[:, :, :], gate_t[:, :, :], zs[:, 2 * i:2 * i + 2, :], ALU.mult).then_inc(gated, 1)

            pair_of = [None]

            def group_mean(G):
                dve.wait_ge(norm_summed, G + 1)
                ts_(mean_sq[:, :], M1[:, 0:SEQ], 1.0 / (4 * 256), EPS, ALU.mult, ALU.add).then_inc(m1_free, 1)

            def group_norm(G):
                dve.wait_ge(rn_ready, G + 1)
                stt_(newton[:, :], rnorm[:, :], -0.5, rnorm[:, :], ALU.mult, ALU.mult).then_inc(newton_step, 1)
                dve.wait_ge(newton_step, 3 * G + 1)
                dve.wait_ge(m1_free, G + 2)
                tt_(newton[:, :], newton[:, :], mean_sq[:, :], ALU.mult).then_inc(newton_step, 1)
                dve.wait_ge(newton_step, 3 * G + 2)
                stt_(rnorm[:, :], newton[:, :], 1.5, rnorm[:, :], ALU.add, ALU.mult).then_inc(newton_step, 1)
                dve.wait_ge(newton_step, 3 * G + 3)
                rb = rnorm[:, :].rearrange("p (o s) -> p o s", o=1).broadcast_to([P, 2, SEQ])
                tt_(gate_n[:, :, :], gate[:, :, :], rb, ALU.mult).then_inc(normed, 1)

            def group_low(G):
                dve.wait_ge(normed, G + 1)
                dve.wait_ge(ssd_hi, G + 1)
                for c in range(2):
                    k = ds(KT + 2 * G + c, 1)
                    ins = stt_(cat_lo[:, k, :], gate_n[:, c:c + 1, :], parB[:, ds(96 + 2 * G + c, 1)],
                               cat_hi[:, k, :].bitcast(f32), ALU.mult, ALU.subtract)
                ins.then_inc(ssd_lo, 1)

            def z_silu(m):
                dve.wait_ge(z_tanh, m + 1)
                stt_(zs[:, :, :], zs[:, :, :], 1.0, tiles(2), ALU.add, ALU.mult).then_inc(z_ready, 1)

            def next_group(G, k):
                if k == 9:
                    silu(G)
                if 8 <= k < 12:
                    decay_args(G, k - 8)

            def ssd_slot(s, m, more=True):
                pair_of[0] = m
                for i, o in enumerate(GROUP_SLOT):
                    G, k = 2 * m + i, s - o
                    if k == 2:
                        mask_cb(G)
                    if 2 <= k < 6:
                        mix_head(G, k - 2)
                    if k == 8:
                        gate_group(G, i)
                    if k == 9:
                        group_mean(G)
                    if k == 10:
                        group_norm(G)
                    if k == 11:
                        group_low(G)
                    if k in CONV_SLOTS and (i == 0 or more):
                        convolve(G + 1, 1 - i, CONV_SLOTS[k])
                    if i == 0 or more:
                        next_group(G + 1, k)
                if s == 2:
                    z_silu(m)

            def qk_sum(n):
                dve.wait_ge(qk_sq, n + 1)
                sq = sq_tmp[:, :, :].rearrange("p t (h e) -> p (t h) e", e=HEAD_DIM)
                dve.tensor_reduce(qk_s[:, 0, :], sq, axis=AX.X, op=ALU.add).then_inc(qk_ss, 1)
                dve.wait_ge(qk_ss, n + 1)
                ts_(qk_s[:, 1, :], qk_s[:, 0, :], 1.0 / HEAD_DIM, EPS, ALU.mult, ALU.add).then_inc(qk_ms, 1)

            def qk_norm(n, i, a):
                dve.wait_ge(qk_rs, n + 1)
                if positive(4 * a):
                    dve.wait_ge(qk_transposed, 4 * a)
                rs = qk_s[:, 2, :].rearrange("p (h o) -> p h o", o=1).broadcast_to([P, 8, HEAD_DIM])
                tt_(qk_n[i][:, :, :].rearrange("p t (h e) -> p (t h) e", e=HEAD_DIM),
                    bank_pair(i).rearrange("p t (h e) -> p (t h) e", e=HEAD_DIM), rs, ALU.mult).then_inc(qk_normed, 1)

            def att_slot(s, g):
                for h in range(4):
                    H = 4 * g + h
                    i = h % 2
                    if s == h + 1:
                        dve.wait_ge(qk_transposed, H + 1)
                        ts_(qkT[:, h, 0, :], (M0, M1)[i][:, 0:SEQ], gqk[:, 0:1], None, ALU.mult)
                        dve.tensor_copy(qkT[:, h, 1, :], (M0, M1)[i][:, SEQ:2 * SEQ]).then_inc(qkT_ready, 1)
                    if s == 5 + 4 * h:
                        dve.wait_ge(scores, H + 1)
                        dve.wait_ge(bias_in[i], 16 * (2 * g + h // 2 + 1))
                        dve.memset(small[:, 40:41], 0.0)
                        for t in range(TT):
                            ins = dve.tensor_tensor_reduce(
                                out=prob[i][:, t, :], in0=M0[:, SEQ * t:SEQ * (t + 1)],
                                in1=bias_t[i][:, P * (1 - t):P * (1 - t) + SEQ], scale=1.0, scalar=-3e38,
                                op0=ALU.add, op1=ALU.max, accum_out=soft[:, i, 0, t:t + 1])
                        ins.then_inc(logits, 1)
                        dve.wait_ge(logits, H + 3)
                        ts_(soft[:, i, 1, :], soft[:, i, 0, :], -1.0, None, ALU.mult).then_inc(neg_max, 1)
                    if s == 6 + 4 * h:
                        dve.wait_ge(probs, H + 1)
                        dve.reciprocal(soft[:, i, 3, :], soft[:, i, 2, :]).then_inc(recip, 1)
                        dve.wait_ge(recip, H + 1)
                        for t in range(TT):
                            ins = ts_(prob[i][:, t, :], prob[i][:, t, :], soft[:, i, 3, t:t + 1], None, ALU.mult)
                        ins.then_inc(p_normed, 1)
                    if s == 10 + 4 * h:
                        dve.wait_ge(att_hi, H + 1)
                        tt_(cat_lo[:, ds(H, 1), :], M1[:, 0:SEQ].rearrange("p (o s) -> p o s", o=1),
                            cat_hi[:, ds(H, 1), :].bitcast(f32), ALU.subtract).then_inc(att_lo, 1)

            for R in range(8):
                x_gain(R, 64)
                if R > 0:
                    x_low(R - 1)
                if R == 3:
                    low(0, 3)
            low(0, 7)
            x_low(7)
            dve.wait_ge(rel_done, 1)
            dve.tensor_copy(relout[:, :], M1[0:HEADS, :]).then_inc(rel_copied, 1)
            dve.wait_ge(dt_hi_ready, 1)
            tt_(dt_lo[:, :, :], dt_raw[:, :, :], dt_hi[:, :, :].bitcast(f32), ALU.subtract).then_inc(dt_lo_ready, 1)
            dve.wait_ge(dt_act, 1)
            ts_(dtcol[:, 4:5], dtcol[:, 2:3], dtcol[:, 3:4], None, ALU.mult).then_inc(dt_step, 1)
            v, e, r, z, z2, p, soft_dt, a_dt = (dtv[n][:, :] for n in ("v", "e", "r", "z", "z2", "p", "soft", "a"))
            step = [1]

            def then_step(ins):
                ins.then_inc(dt_step, 1)
                step[0] += 1
                dve.wait_ge(dt_step, step[0])

            def dt_softplus():
                dve.wait_ge(dt_done, 1)
                ts_(v, M0[0:64, 0:SEQ], dtcol[:, 0:1], None, ALU.add).then_inc(m0_free, 1)
                dve.wait_ge(m0_free, 1)
                then_step(stt_(e, v, -1.0, v, ALU.mult, ALU.max))
                dve.wait_ge(dt_act, 2)
                then_step(ts_(r, e, 2.0, None, ALU.add))
                then_step(dve.reciprocal(r, r))
                then_step(tt_(z, e, r, ALU.mult))
                then_step(tt_(z2, z, z, ALU.mult))
                then_step(ts_(p, z2, 1.0 / 17, None, ALU.mult))
                for k in (15, 13, 11, 9, 7, 5, 3):
                    then_step(stt_(p, p, 1.0 / k, z2, ALU.add, ALU.mult))
                then_step(stt_(p, p, 1.0, z, ALU.add, ALU.mult))
                then_step(ts_(r, v, 0.0, None, ALU.max))
                then_step(stt_(soft_dt, p, 2.0, r, ALU.mult, ALU.add))
                then_step(ts_(a_dt, soft_dt, dtcol[:, 4:5], None, ALU.mult))

            def dt_sums():
                for c in range(TT):
                    then_step(dve.tensor_tensor_scan(prefix[:, c, 1:P + 1], one_row[:, :], a_dt[:, P * c:P * (c + 1)],
                                                     0.0, ALU.mult, ALU.add))
                F, B = slice(0, 32), slice(32, 64)
                for c in range(TT):
                    ts_(dt_rows[F, c, :], prefix[F, c, 1:P + 1], -1.0, None, ALU.mult)
                    ts_(dt_rows[B, c, :], prefix[B, c, 0:P], -1.0, None, ALU.mult)
                    dve.tensor_copy(dt_rows[:, 3 + c, :], soft_dt[:, P * c:P * (c + 1)])
                ts_(dt_rows[F, 2, :], prefix[F, 0, 1:P + 1], -1.0, prefix[F, 0, P:P + 1], ALU.mult, ALU.add)
                then_step(ts_(dt_rows[B, 2, :], prefix[B, 1, 0:P], -1.0, prefix[B, 0, P:P + 1], ALU.mult, ALU.subtract))

            def dt_tokens():
                dve.wait_ge(dt_tok, 1)
                dve.tensor_copy(tokp[:, :, :].rearrange("p a h -> p (a h)"), M1[:, 0:320]).then_inc(m1_free, 1)

            for s in range(CH - LEAD, WIN):
                low_ahead(0, s)
                if s == 6:
                    dt_softplus()
                if s == 8:
                    dt_sums()
                if s == 13:
                    dt_tokens()
                if s - GROUP_SLOT[1] in CONV_SLOTS:
                    if s - GROUP_SLOT[1] == 0:
                        dve.wait_ge(params_ready, 8)
                    convolve(0, 0, CONV_SLOTS[s - GROUP_SLOT[1]])
                next_group(0, s - GROUP_SLOT[1])
            dve.wait_ge(pool_masks, 5)
            dve.wait_ge(m1_free, 1)
            dve.wait_ge(params_ready, 8)

            def ssd_window(w, m):
                for s in range(WIN):
                    low_ahead(3 * w, s)
                    ssd_slot(s, m)

            def att_window(a, m, g):
                for s in range(WIN):
                    low_ahead(12 + 3 * a, s)
                    if m is not None:
                        ssd_slot(s, m, False)
                    if g is not None:
                        att_slot(s, g)
                    for i in range(2):
                        if s == 10 + 8 * i:
                            qk_sum(2 * a + i)
                        if s == 12 + 8 * i:
                            qk_norm(2 * a + i, i, a)

            with dve.Fori(1, 4) as w:
                ssd_window(w, w - 1)
            att_window(0, 3, None)
            with dve.Fori(1, 4) as a:
                att_window(a, None, a - 1)

            def out_add(n):
                dve.wait_ge(chunk_used, CH * (OUT_U + n + 1))
                dve.wait_ge(xres_in, 32)
                if n < 4:
                    tt_(xres[:, n], bank_pair((0, 1, 2, 0)[n]), xres[:, n], ALU.add).then_inc(added, 1)
                else:
                    tt_(acc[:, n - 4], bank_pair((1, 2, 0, 1)[n - 4]), xres[:, n - 4], ALU.add).then_inc(added, 1)

            def mid_block(b):
                for R in (8 + 2 * b, 9 + 2 * b):
                    x_gain(R, 80)
                for R in (8 + 2 * b, 9 + 2 * b):
                    x_low(R)

            for n in range(8):
                for j in range(CH):
                    s = CH * n + j
                    low_ahead(OUT_U, s)
                    att_slot(s, 3)
                    if n > 0 and j == 2:
                        out_add(n - 1)
                    if n > 4 and j == 4:
                        mid_block(n - 5)
            out_add(7)
            mid_block(3)
            dve.wait_ge(squared_mid, 8)
            dve.tensor_reduce(inv_ms[:, 0, :], ssum[:, :, :], axis=AX.X, op=ALU.add).then_inc(mid_step, 1)
            dve.wait_ge(mid_step, 1)
            ts_(inv_ms[:, 1, :], inv_ms[:, 0, :], 1.0 / D_MODEL, EPS, ALU.mult, ALU.add).then_inc(mid_step, 1)
            dve.wait_ge(mid_step, 2)
            dve.reciprocal(inv_ms[:, 2, :], inv_ms[:, 1, :]).then_inc(mid_step, 1)
            dve.wait_ge(mid_step, 3)

            def relu_square(n, q):
                dve.wait_ge(relu_done, 4 * q + n + 1)
                if positive(4 * q + n):
                    dve.wait_ge(hid_hi_s, 4 * q + n)
                if positive(4 * q + n):
                    dve.wait_ge(hid_lo_s, 4 * q + n)
                tt_(relu_sq[:, :, :], relu_t[:, :, :], relu_t[:, :, :], ALU.mult).then_inc(relu_squared, 1)

            def hid_low(n, q):
                dve.wait_ge(hid_hi_s, 4 * q + n + 1)
                tt_(hid_lo[:, 4 * n:4 * n + 4, :], relu_sq[:, :, :], hid_hi[:, 4 * n:4 * n + 4, :].bitcast(f32),
                    ALU.subtract).then_inc(hid_lo_s, 1)

            def down_add(U, n, q):
                dve.wait_ge(chunk_used, CH * (U + 1))
                if positive(4 * (q - 1) + n + 1):
                    dve.wait_ge(down_added, 4 * (q - 1) + n + 1)
                for t in range(TT):
                    ins = stt_(acc[:, n, t, :], bank_pair(n)[:, t, :], inv_ms[:, 2, t:t + 1], acc[:, n, t, :],
                               ALU.mult, ALU.add)
                ins.then_inc(down_added, 1)

            def mlp_quarter(q):
                for s in range(8 * CH):
                    n, j = divmod(s, CH)
                    if j in DVE_CHUNKS:
                        low(MLP_U + 8 * q + n, j)
                    if 1 <= n <= 4 and j == 2:
                        relu_square(n - 1, q)
                    if 1 <= n <= 4 and j == 3:
                        hid_low(n - 1, q)
                    if n >= 5 and j == 2:
                        down_add(MLP_U + 8 * q + n - 1, n - 5, q)
                down_add(MLP_U + 8 * q + 7, 3, q)

            mlp_quarter(0)
            with dve.Fori(1, 4) as q:
                mlp_quarter(q)

        @block.tensor
        def _(pe):
            def mm(o, lhsT, rhs, first, last, **kw):
                return pe.matmul(o, lhsT, rhs, start=first, stop=last, **kw)

            pe.sem_inc(y_done, PER_GROUP)

            def chunk_by_weights(U, j, pair, skip=False):
                wait_low(pe, U, j)
                i = j % RING
                res = tiles(pair)
                for kk in range(KC):
                    k = KC * j + kk
                    for c in range(4):
                        cols = slice(P * c, P * c + P)
                        for n, (w, a) in enumerate(((w_hi, actT_lo), (w_lo, actT_hi), (w_hi, actT_hi))):
                            ins = mm(res[:, c, :], w[i][:, kk, cols], a[:, k, :],
                                     k == 0 and n == 0 and c % 2 == 0,
                                     k == KT - 1 and n == 2, skip_group_check=True)
                ins.then_inc(chunk_used, 1)

            def chunk_by_tokens(U, j, pair, hi, lo, k0):
                wait_low(pe, U, j)
                i = j % RING
                for kk in range(KC):
                    k = KC * j + kk
                    for t in range(TT):
                        toks = slice(P * t, P * t + P)
                        for n, (a, w) in enumerate(((lo, w_hi), (hi, w_lo), (hi, w_hi))):
                            ins = mm(bank_pair(pair)[:, t, :], a[:, k0 + k, toks], w[i][:, kk, :],
                                     k == 0 and n == 0, k == KT - 1 and n == 2)
                ins.then_inc(chunk_used, 1)

            def rows_round(R):
                r = R % 8
                bank = (M0, M1)[R % 2]
                if positive(R - 1):
                    pe.wait_ge(xg_ready, R - 1)
                for kk in range(KC):
                    for t in range(TT):
                        k = KC * r + kk
                        src = (x_in[:, t, P * k:P * k + P] if R < 8 else
                               acc[:, k // 4, t, P * (k % 4):P * (k % 4) + P])
                        ins = pe.transpose(bank[:, SEQ * kk + P * t:SEQ * kk + P * t + P], src, ident[:, :])
                ins.then_inc(xt_done, 1)

            def ssd_slot(s, m):
                for i, o in enumerate(GROUP_SLOT):
                    G, k = 2 * m + i, s - o
                    if k == 1:
                        pe.wait_ge(xbc_ready, G + 1)
                        pe.wait_ge(m0_free, G + 1)
                        for t in range(TT):
                            for c in range(2):
                                ins = pe.transpose(M0[:, SEQ * t + P * c:SEQ * t + P * c + P],
                                                   xbc[:, c, P * t:P * t + P], ident[:, :])
                        ins.then_inc(x_transposed, 1)
                        pe.wait_ge(m1_free, G + 1)
                        for t in range(TT):
                            ins = mm(M1[:, SEQ * t:SEQ * (t + 1)], xbc[:, 2, P * t:P * t + P], xbc[:, 3, :], True, True)
                        ins.then_inc(cb_done, 1)
                    if k in (5, 7):
                        pe.wait_ge(xtok_ready, G + 1)
                        pe.wait_ge(mix_ready, 4 * G + k - 3)
                        for t in range(TT):
                            for h in (k - 5, k - 4):
                                ins = mm(M0[64 * (h % 2):64 * (h % 2) + 64, SEQ * (h // 2):SEQ * (h // 2 + 1)],
                                         xtok[:, t, 64 * h:64 * h + 64], mix[h][:, 4 * t:4 * t + 2, :],
                                         t == 0, t == TT - 1)
                                if t == TT - 1:
                                    ins.then_inc(y_done, 1)
                    if k == 9:
                        pe.wait_ge(gate_squared, G + 1)
                        pe.wait_ge(cb_masked, G + 1)
                        for c in range(2):
                            ins = mm(M1[:, 0:SEQ], ones[:, :], gate_sq[:, c, :], c == 0, c == 1)
                        ins.then_inc(norm_summed, 1)

            def att_slot(s, g):
                for h in range(4):
                    H = 4 * g + h
                    if s == h:
                        pe.wait_ge(qk_normed, 2 * g + 2)
                        if h == 0:
                            pe.wait_ge(m0_free, 9)
                            pe.wait_ge(logits, 4 * g + 2)
                        if h == 1:
                            pe.wait_ge(m1_free, 9)
                            pe.wait_ge(att_lo, 4 * g + 1)
                        if h > 1:
                            pe.wait_ge(qkT_ready, H - 1)
                        for n in range(2):
                            for t in range(TT):
                                ins = pe.transpose((M0, M1)[h % 2][:, SEQ * n + P * t:SEQ * n + P * t + P],
                                                   qk_n[n][:, t, P * h:P * h + P], ident[:, :])
                        ins.then_inc(qk_transposed, 1)
                    if s == 4 + 4 * h:
                        pe.wait_ge(qkT_ready, 4 * g + max(h + 1, 3))
                        if h > 0:
                            pe.wait_ge(logits, H + 2)
                        for t in range(TT):
                            ins = mm(M0[:, SEQ * t:SEQ * (t + 1)], qkT[:, h, 0, P * t:P * t + P], qkT[:, h, 1, :],
                                     True, True)
                        ins.then_inc(scores, 1)
                    if s == 7 + 4 * h:
                        pe.wait_ge(p_normed, H + 1)
                        if h == 0:
                            pe.wait_ge(qkT_ready, 4 * g + 4)
                        else:
                            pe.wait_ge(att_lo, H + 1)
                        for n in range(TT):
                            for t in range(TT):
                                ins = pe.transpose(M1[:, SEQ * n + P * t:SEQ * n + P * t + P],
                                                   prob[h % 2][:, t, P * n:P * n + P], ident[:, :])
                        ins.then_inc(p_transposed, 1)
                    if s == 9 + 4 * h:
                        pe.wait_ge(pT_ready, H + 1)
                        pe.wait_ge(v_copied, g + 1)
                        for n in range(TT):
                            ins = mm(M1[:, 0:SEQ], v_tok[:, n, P * h:P * h + P], probT[:, n, :], n == 0, n == TT - 1)
                        ins.then_inc(pv_done, 1)

            pe.wait_ge(pool_masks, 1)
            pe.wait_ge(consts, 11)
            pe.wait_ge(rows_in, 128)
            pe.transpose(M0[:, 0:P], rowsA[:, :], ident[:, :])
            pe.transpose(M0[:, P:P + 114], rowsB[:, :], ident[0:114, 0:114]).then_inc(params_t, 1)
            pe.wait_ge(x_scaled, 1)
            pe.wait_ge(x_scaled_act, 1)
            pe.wait_ge(params_ready, 2)
            for R in range(3):
                rows_round(R)

            def dt_unit():
                pe.wait_ge(xg_ready, 8)
                pe.wait_ge(dt_lo_ready, 1)
                for k in range(KT):
                    for n, (w, a) in enumerate(((dt_hi, actT_lo), (dt_lo, actT_hi), (dt_hi, actT_hi))):
                        ins = mm(M0[0:64, 0:SEQ], w[:, k, :], a[:, k, :], k == 0 and n == 0, k == KT - 1 and n == 2)
                ins.then_inc(dt_done, 1)

            for s in range(WIN):
                r, j = divmod(s, CH)
                if s < CH:
                    pe.wait_ge(xl_ready, j + 1)
                chunk_by_weights(r, j, r)
                if s + 3 < CH:
                    rows_round(s + 3)
                if s == 5:
                    pe.wait_ge(relw_in, 32)
                    pe.wait_ge(xg_ready, 8)
                    mm(M1[0:HEADS, :], relw[:, :], reltab[:, :], True, True).then_inc(rel_done, 1)
                if s == 6:
                    dt_unit()
                if s == 12:
                    pe.wait_ge(rel_copied, 1)
                    pe.wait_ge(dt_step, DT_STEPS)
                    for i in range(5):
                        ins = pe.transpose(M1[:, 64 * i:64 * i + 64], dt_rows[:, i, :], ident[0:64, 0:64])
                    ins.then_inc(dt_tok, 1)

            def ssd_window(w, m):
                for s in range(WIN):
                    r, j = divmod(s, CH)
                    if j == 0:
                        if r < 2:
                            pe.wait_ge(xbc_in, 2 * (w - 1) + r + 1)
                        else:
                            pe.wait_ge(z_ready, w)
                    chunk_by_weights(3 * w + r, j, r)
                    ssd_slot(s, m)

            def att_window(a, m, g):
                for s in range(WIN):
                    r, j = divmod(s, CH)
                    if j == 0:
                        if m is not None:
                            pe.wait_ge((xbc_in, xbc_in, z_ready)[r], (7, 8, 4)[r])
                        elif r < 2:
                            pe.wait_ge(qk_normed, 2 * (a - 1) + r + 1)
                        else:
                            pe.wait_ge(v_copied, a)
                    chunk_by_tokens(12 + 3 * a + r, j, r, actT_hi, actT_lo, 0)
                    if m is not None:
                        ssd_slot(s, m)
                    if g is not None:
                        att_slot(s, g)

            with pe.Fori(1, 4) as w:
                ssd_window(w, w - 1)
            att_window(0, 3, None)
            with pe.Fori(1, 4) as a:
                att_window(a, None, a - 1)
            for n in range(8):
                pair = (0, 1, 2, 0, 1, 2, 0, 1)[n]
                for j in range(CH):
                    s = CH * n + j
                    if j == 0:
                        if n < 2:
                            pe.wait_ge(qk_normed, 6 + n + 1)
                        elif n == 2:
                            pe.wait_ge(v_copied, 4)
                        else:
                            pe.wait_ge(added, n - 2)
                    if n == 0 and j == 0:
                        pe.wait_ge(ssd_lo, 8)
                    if n == 4:
                        pe.wait_ge(att_lo, 2 * j + 3)
                    chunk_by_tokens(OUT_U + n, j, pair, cat_hi, cat_lo, KT * (1 - n // 4))
                    att_slot(s, 3)
                    if n > 4 and j == 3:
                        pe.wait_ge(added, n)
                        pe.wait_ge(logits, 18)
                        rows_round(8 + 2 * (n - 5))
                        rows_round(9 + 2 * (n - 5))
            pe.wait_ge(added, 8)
            rows_round(14)
            rows_round(15)

            def mlp_quarter(q, first):
                for n in range(4):
                    for j in range(CH):
                        if j == 0:
                            if first:
                                if n == 3:
                                    pe.wait_ge(xg_ready, 16)
                                else:
                                    pe.wait_ge(added, 8)
                            else:
                                if positive(4 * (q - 1) + n + 1):
                                    pe.wait_ge(down_added, 4 * (q - 1) + n + 1)
                        if first and n == 0:
                            pe.wait_ge(xl_ready, 8 + j + 1)
                        chunk_by_weights(MLP_U + 8 * q + n, j, n)
                for n in range(4):
                    for j in range(CH):
                        if j == 0:
                            pe.wait_ge(relu_done, 4 * q + n + 1)
                        if n == 0 and j % 2 == 0:
                            pe.wait_ge(hid_lo_s, 4 * q + j // 2 + 1)
                        chunk_by_tokens(MLP_U + 8 * q + 4 + n, j, n, hid_hi, hid_lo, 0)

            mlp_quarter(0, True)
            with pe.Fori(1, 4) as q:
                mlp_quarter(q, False)


DT_STEPS = 21


_INS = ["x", "norm_mix_g", "w_in", "q_norm_g", "k_norm_g", "rel_bias", "conv_w", "conv_b", "dt_bias", "a_log",
        "d_skip", "ssd_norm_g", "w_out", "norm_mlp_g", "w_up", "w_down"]


def kernel(**inputs):
    import concourse.bacc as bacc
    from concourse.bass_utils import run_bass_kernel_spmd

    nc = bacc.Bacc("TRN2", target_bir_lowering=False, num_devices=1)
    arrays, args = {}, []
    for name in _INS:
        a = np.ascontiguousarray(inputs[name])
        arrays[f"in_{name}"] = a
        args.append(nc.dram_tensor(f"in_{name}", a.shape, mybir.dt.from_np(a.dtype), kind="ExternalInput").ap())
    table = bias_constants()
    arrays["bias_table"] = table
    args.append(nc.dram_tensor("bias_table", table.shape, mybir.dt.float32, kind="ExternalInput").ap())
    out = nc.dram_tensor("out", (1, SEQ, D_MODEL), mybir.dt.float32, kind="ExternalOutput").ap()
    build(nc, *args, out)
    r = run_bass_kernel_spmd(nc, [arrays], core_ids=[0])
    return r.results[0]["out"]
```

```python
import math
from contextlib import ExitStack

import numpy as np

import concourse.bass as bass
from concourse import mybir

P = 128
SEQ, D_MODEL = 256, 2048
HEADS, HEAD_DIM = 16, 128
SSM_HEADS, GROUPS = 32, 8
PER_GROUP = SSM_HEADS // GROUPS
BUCKETS = 32
EPS = 1e-6
PATTERNS = ((128, 1), (512, 4), (2048, 16))

TT = SEQ // P
UNIT = 512
KT = 16
CH = 8
KC = KT // CH
RING = 4
X_SPLIT = 1280
DVE_CHUNKS = (3, 7)
POOL_CHUNKS = tuple(j for j in range(CH) if j not in DVE_CHUNKS)
WIN = 3 * CH
LEAD = 3
COL_Q, COL_K, COL_V, COL_Z, COL_X = 0, 2048, 4096, 6144, 8192
COL_B, COL_C, COL_DT = 10240, 11264, 12288
GROUP_SLOT = (0, 12)
CONV_SLOTS = {0: (0, 1), 1: (2,), 6: (3,), 7: (4,)}
DT_STEPS = 21
ROW = 384


def t5_bucket(rel):
    nb = BUCKETS // 2
    max_exact = nb // 2
    n = np.abs(rel)
    nf = np.maximum(n, 1).astype(np.float32)
    large = max_exact + (np.log(nf / np.float32(max_exact)) / np.float32(math.log(1024 / max_exact))
                         * np.float32(nb - max_exact)).astype(np.int32)
    return (rel > 0) * nb + np.where(n < max_exact, n, np.minimum(large, nb - 1))


def bias_constants():
    rel = np.arange(512) - (SEQ - 1)
    table = np.zeros((BUCKETS + 1, 512), np.float32)
    table[t5_bucket(rel), np.arange(512)] = 1.0
    count = sum(((np.abs(rel) <= window // 2) & (rel % step == 0)).astype(int) for window, step in PATTERNS)
    table[BUCKETS] = np.where(count > 0, np.log(np.maximum(count, 1)), -1e30)
    return table


def build(nc, x, norm_mix_g, w_in, q_norm_g, k_norm_g, rel_bias, conv_w, conv_b, dt_bias, a_log,
          d_skip, ssd_norm_g, w_out, norm_mlp_g, w_up, w_down, bias_table, out):
    f32, f32r = mybir.dt.float32, mybir.dt.float32r
    ALU, ACT, AX = mybir.AluOpType, mybir.ActivationFunctionType, mybir.AxisListType
    ds = bass.ds
    ctx = ExitStack()

    w_in_v = w_in[0].rearrange("(t p) n -> p t n", p=P)
    w_out_v = w_out[0].rearrange("(t p) n -> p t n", p=P)
    w_up_v = w_up[0].rearrange("(t p) n -> p t n", p=P)
    w_down_v = w_down[0].rearrange("(t p) n -> p t n", p=P)
    x_v = x[0].rearrange("(t p) (n c) -> p t n c", p=P, c=UNIT)
    out_v = out[0].rearrange("(t p) (n c) -> p t n c", p=P, c=UNIT)
    rel_rows = nc.dram_tensor("rel_rows", [HEADS, 512], f32).ap()
    rel_tiles = nc.dram_tensor("rel_tiles", [P, HEADS, ROW], f32).ap()
    decay_rows = nc.dram_tensor("decay_rows", [64, SEQ], f32).ap()

    with ctx:
        words = (nc.sbuf_usable_end - nc.sbuf_base - 64) // 32 * 8
        ctx.enter_context(nc.sbuf_tensor("arena", [P, words], f32))
        end = nc.sbuf_base
        top = [end - 4 * words]

        def place(name, shape, dt=f32, at=None):
            size = 4 * int(np.prod(shape[1:]))
            offset = top[0] if at is None else at
            if at is None:
                top[0] += (size + 31) // 32 * 32
                assert top[0] <= end, (name, top[0], end)
            return nc.alloc_sbuf_tensor_at(name, shape, dt, offset=offset)

        act_base = top[0]
        actT_hi = place("actT_hi", [P, KT, SEQ], f32r)
        actT_lo = place("actT_lo", [P, KT, SEQ], f32r)
        xres = place("xres", [P, 4, TT, UNIT], f32, at=act_base)
        cat_base = top[0]
        cat_hi = place("cat_hi", [P, 2 * KT, SEQ], f32r)
        cat_lo = place("cat_lo", [P, 2 * KT, SEQ], f32r)
        hid_hi = place("hid_hi", [P, KT, SEQ], f32r, at=cat_base)
        hid_lo = place("hid_lo", [P, KT, SEQ], f32r, at=cat_base + KT * SEQ * 4)
        raw = [place(f"raw{j}", [P, KC, UNIT]) for j in range(CH)]
        w_hi = [place(f"w_hi{j}", [P, KC, UNIT], f32r) for j in range(RING)]
        w_lo = [place(f"w_lo{j}", [P, KC, UNIT], f32r) for j in range(RING)]
        ident = place("ident", [P, P])
        ones = place("ones", [P, P])
        ones_r = place("ones_r", [P, P], f32r)
        parA = place("parA", [P, P])
        parB = place("parB", [P, 114])
        gqk = place("gqk", [P, 1])
        small = place("small", [P, 48])
        halfneg = place("halfneg", [P, 8])
        dskip = place("dskip", [P, 16])
        dskip_all = place("dskip_all", [P, SSM_HEADS])
        tokp = place("tokp", [P, 5, 64])
        phase = top[0]

        x_in = place("x_in", [P, TT, D_MODEL], at=cat_base)
        squares_act = place("squares_act", [P, D_MODEL], at=cat_base + 16384)
        rowsA = place("rowsA", [P, P], at=cat_base + 24576)
        rowsB = place("rowsB", [114, P], at=cat_base + 25088)
        relw = place("relw", [BUCKETS + 1, HEADS], at=cat_base + 25600)
        reltab = place("reltab", [BUCKETS + 1, 512], at=cat_base + 25664)
        relout = place("relout", [HEADS, 512], at=cat_base + 27712)
        squares_dve = place("squares_dve", [P, D_MODEL], at=phase + 16384)
        rs_row = place("rs_row", [P, SEQ], at=phase + 24576)
        rs_diag = place("rs_diag", [P, TT, P], at=phase + 25600)
        xg = [place(f"xg{i}", [P, KC, SEQ], at=phase + 2048 * i) for i in range(2)]

        def at_of(cursor, size):
            offset = cursor[0]
            cursor[0] += size
            return offset

        lo1 = [cat_base + 32768]
        dt_raw = place("dt_raw", [P, KT, 64], at=at_of(lo1, 4096))
        dt_hi = place("dt_hi", [P, KT, 64], f32r, at=at_of(lo1, 4096))
        dt_lo = place("dt_lo", [P, KT, 64], f32r, at=at_of(lo1, 4096))
        lo2 = [cat_base + 32768]
        lo3 = [cat_base]
        gate_t = place("gate_t", [P, 2, SEQ], at=at_of(lo2, 2048))
        gate = place("gate", [P, 2, SEQ], at=at_of(lo2, 2048))
        gate_sq = place("gate_sq", [P, 2, SEQ], at=at_of(lo2, 2048))
        xtok = place("xtok", [P, TT, SEQ], at=at_of(lo2, 2048))
        mean_sq = place("mean_sq", [P, SEQ], at=at_of(lo2, 1024))
        log_ms = place("log_ms", [P, SEQ], at=at_of(lo2, 1024))
        rnorm = place("rnorm", [P, SEQ], at=at_of(lo2, 1024))
        newton = place("newton", [P, SEQ], at=at_of(lo2, 1024))
        sq_hi = place("sq_hi", [P, 2, SEQ], f32r, at=cat_base + 32768)
        sq_lo = place("sq_lo", [P, 2, SEQ], f32r, at=lo2[0] - 3072)
        gate_n = gate_t
        hi1 = [phase + 4096]
        mask = place("mask", [P, 6, P], at=at_of(hi1, 3072))
        cbm = place("cbm", [P, 6, P], at=at_of(hi1, 3072))
        mix = [place(f"mix{i}", [P, 6, P], at=at_of(hi1, 3072)) for i in range(PER_GROUP)]
        decay = place("decay", [P, 2, PER_GROUP, SEQ], at=at_of(hi1, 8192))
        zs = place("zs", [P, 4, SEQ], at=at_of(hi1, 4096))
        conv_in = place("conv_in", [P, 2, 4, SEQ + 4], at=at_of(hi1, 8320))
        assert hi1[0] <= end, (hi1[0], end)
        conv = place("conv", [P, 4, SEQ], at=at_of(lo3, 4096))
        conv_t = place("conv_t", [P, 4, SEQ], at=at_of(lo3, 4096))
        xbc = place("xbc", [P, 4, SEQ], at=at_of(lo3, 4096))
        lo4 = [cat_base + 32768 + 16384]
        dtv = {n: place("dt_" + n, [64, SEQ], at=at_of(lo4, 1024))
               for n in ("v", "e", "r", "z", "z2", "p", "soft", "a")}
        prefix = place("prefix", [64, TT, P + 1], at=at_of(lo4, 1088))
        dt_rows = place("dt_rows", [64, 5, P], at=at_of(lo4, 2560))
        dtcol = place("dtcol", [64, 8], at=at_of(lo4, 64))
        one_row = place("one_row", [64, P], at=at_of(lo4, 512))

        qk_n = [place(n, [P, TT, UNIT], at=cat_base + 32768 * i + 12288) for i, n in enumerate(("q_n", "k_n"))]
        att = [phase]
        sq_tmp = place("sq_tmp", [P, TT, UNIT], at=at_of(att, 4096))
        v_hi, v_lo = (place(n, [P, TT, UNIT], f32r, at=at_of(att, 4096)) for n in ("v_hi", "v_lo"))
        qkT_hi, qkT_lo = (place(n, [P, 4, 2, SEQ], f32r, at=at_of(att, 8192)) for n in ("qkT_hi", "qkT_lo"))
        bias_t = [place(f"bias_t{i}", [P, ROW], at=at_of(att, 4 * ROW)) for i in range(2)]
        prob = [place(f"prob{i}", [P, TT, SEQ], at=at_of(att, 2048)) for i in range(2)]
        pT_hi, pT_lo = (place(n, [P, TT, SEQ], f32r, at=at_of(att, 2048)) for n in ("pT_hi", "pT_lo"))
        soft = place("soft", [P, 2, 4, TT], at=at_of(att, 64))
        qk_s = small[:, 8:32].rearrange("p (a h) -> p a h", a=3)
        assert att[0] <= end
        mlp = [phase + 4096]
        acc = place("acc", [P, 4, TT, UNIT], at=at_of(mlp, 16384))
        sq_junk = place("sq_junk", [P, UNIT], at=at_of(mlp, 2048))
        relu_t = place("relu_t", [P, 4, SEQ], at=at_of(mlp, 4096))
        relu_sq = place("relu_sq", [P, 4, SEQ], at=at_of(mlp, 4096))
        ssum = place("ssum", [P, TT, 4], at=at_of(mlp, 32))
        inv_ms = place("inv_ms", [P, 3, TT], at=at_of(mlp, 32))
        assert mlp[0] <= end

        psum = ctx.enter_context(nc.psum_tensor("psum", [P, 8, UNIT], f32))
        M0, M1 = psum[:, 6, :], psum[:, 7, :]

        def bank_pair(n):
            return psum[:, 2 * n:2 * n + 2, :]

        def tiles(n):
            return bank_pair(n).rearrange("p b (t s) -> p (b t) s", t=2)

        def sem(name):
            return ctx.enter_context(nc.semaphore(name))

        raw_in = [sem(f"raw_in{j}") for j in range(CH)]
        hi_ready, lo_pool, lo_dve, chunk_used = sem("hi_ready"), sem("lo_pool"), sem("lo_dve"), sem("chunk_used")
        x_in_s = [sem(f"x_in{t}") for t in range(TT)]
        table_in, ones_rounded, sq_high, sq_low = (sem(n) for n in ("table_in", "ones_rounded", "sq_high", "sq_low"))
        rows_in, relw_in, col_in, dtw_in, dskip_in = (sem(n) for n in (
            "rows_in", "relw_in", "col_in", "dtw_in", "dskip_in"))
        consts, pool_masks = sem("consts"), sem("pool_masks")
        x_sq, x_sq_dve, x_ms, x_rs, rs_diagonal, rs_spread, rs_row_in = (sem(n) for n in (
            "x_sq", "x_sq_dve", "x_ms", "x_rs", "rs_diagonal", "rs_spread", "rs_row_in"))
        params_t, params_ready, rel_done, rel_copied, rel_stored = (sem(n) for n in (
            "params_t", "params_ready", "rel_done", "rel_copied", "rel_stored"))
        xt_done, xg_ready, xh_ready, xl_ready = (sem(n) for n in ("xt_done", "xg_ready", "xh_ready", "xl_ready"))
        dt_hi_ready, dt_lo_ready, dt_done, dt_act, dt_step, dt_tok, decay_stored = (sem(n) for n in (
            "dt_hi_ready", "dt_lo_ready", "dt_done", "dt_act", "dt_step", "dt_tok", "decay_stored"))
        m0_free, m1_free = sem("m0_free"), sem("m1_free")
        xbc_in, conv_step, conv_tanh, xbc_ready = (sem(n) for n in (
            "xbc_in", "conv_step", "conv_tanh", "xbc_ready"))
        decay_in = sem("decay_in")
        args_ready, decays_ready, scaled, mix_ready, y_done = (sem(n) for n in (
            "args_ready", "decays_ready", "scaled", "mix_ready", "y_done"))
        x_transposed, xtok_ready, cb_done, cb_masked = (sem(n) for n in (
            "x_transposed", "xtok_ready", "cb_done", "cb_masked"))
        gated, gate_squared, norm_summed, ln_ready, rn_ready, newton_step, normed, ssd_hi, ssd_lo = (sem(n) for n in (
            "gated", "gate_squared", "norm_summed", "ln_ready", "rn_ready", "newton_step", "normed", "ssd_hi", "ssd_lo"))
        z_tanh, z_ready = sem("z_tanh"), sem("z_ready")
        qk_sq, qk_ss, qk_ms, qk_rs, qk_normed, v_high, v_low = (sem(n) for n in (
            "qk_sq", "qk_ss", "qk_ms", "qk_rs", "qk_normed", "v_high", "v_low"))
        bias_in = [sem(f"bias_in{i}") for i in range(2)]
        qk_transposed, qkT_ready, scores, logits, neg_max, probs, recip, p_normed = (sem(n) for n in (
            "qk_transposed", "qkT_ready", "scores", "logits", "neg_max", "probs", "recip", "p_normed"))
        qkT_high, pT_high = sem("qkT_high"), sem("pT_high")
        p_transposed, pT_ready, pv_done, att_hi, att_lo = (sem(n) for n in (
            "p_transposed", "pT_ready", "pv_done", "att_hi", "att_lo"))
        xres_in, added, squared_mid, mid_step = sem("xres_in"), sem("added"), sem("squared_mid"), sem("mid_step")
        relu_done, relu_squared, hid_hi_s, hid_lo_s, down_added, out_stored = (sem(n) for n in (
            "relu_done", "relu_squared", "hid_hi_s", "hid_lo_s", "down_added", "out_stored"))

        block = ctx.enter_context(nc.Block())

        def positive(count):
            return not isinstance(count, int) or count > 0

        def wait_low(eng, U, j):
            if j in DVE_CHUNKS:
                eng.wait_ge(lo_dve, len(DVE_CHUNKS) * U + DVE_CHUNKS.index(j) + 1)
            else:
                eng.wait_ge(lo_pool, len(POOL_CHUNKS) * U + POOL_CHUNKS.index(j) + 1)

        MIX_UNITS = 24
        OUT_U = MIX_UNITS
        MLP_U = OUT_U + 8

        @block.sync
        def _(sp):
            def load(U, j, pieces):
                if positive(U):
                    wait_low(sp, U - 1, j)
                at = 0
                for src in pieces:
                    n = src.shape[-1]
                    sp.dma_start(raw[j][:, :, at:at + n], src).then_inc(raw_in[j], 16 * len_of[len(pieces)])
                    at += n

            len_of = {1: 3, 3: 1}

            def in_cols(j, c0, n=UNIT):
                return w_in_v[:, KC * j:KC * (j + 1), ds(c0, n)]

            def ssd_window(w, m):
                for s in range(WIN):
                    r, j = divmod(s, CH)
                    if r < 2:
                        g = 2 * w + r
                        load(3 * w + r, j, [in_cols(j, COL_X + 256 * g, 256), in_cols(j, COL_B + 128 * g, 128),
                                            in_cols(j, COL_C + 128 * g, 128)])
                        if m is None and s == 5:
                            sp.dma_start(dt_raw[:, :, :], w_in_v[:, :, COL_DT:COL_DT + 64]).then_inc(dtw_in, 16)
                            sp.dma_start(dtcol[:, 0:1], dt_bias[0].rearrange("d (h o) -> (d h) o", o=1)).then_inc(col_in, 16)
                            sp.dma_start(dtcol[:, 1:2], a_log[0].rearrange("d (h o) -> (d h) o", o=1)).then_inc(col_in, 16)
                            sp.dma_start(dskip_all[:, :], d_skip[0:1, :].broadcast_to([P, SSM_HEADS])).then_inc(dskip_in, 16)
                    else:
                        load(3 * w + r, j, [in_cols(j, COL_Z + UNIT * w)])
                    decay_loads(s, w, m)

            def load_decay(g):
                src = decay_rows.rearrange("(d h) s -> d h s", d=2)[:, ds(PER_GROUP * g, PER_GROUP), :]
                for d in range(2):
                    sp.dma_start(decay[:, d], src[d:d + 1].broadcast_to([P, PER_GROUP, SEQ])).then_inc(decay_in, 16)

            def decay_loads(s, w, m):
                if s == 13 and m is not None:
                    sp.wait_ge(args_ready, 8 * m + 4)
                    load_decay(2 * m + 1)
                if s == 23 and w is not None:
                    if positive(w):
                        sp.wait_ge(args_ready, 8 * w)
                    else:
                        sp.wait_ge(decay_stored, 32)
                    load_decay(2 * w)

            def load_bias(s, g):
                if s in (10, 14, 18, 22):
                    h = (s - 10) // 4
                    sp.wait_ge(logits, 4 * g + h + 1)
                    sp.dma_start(bias_t[h % 2][:, :].rearrange("p (o j) -> p o j", o=1),
                                 rel_tiles[:, ds(4 * g + h, 1), :]).then_inc(bias_in[h % 2], 16)

            def att_window(a, m, g):
                for s in range(WIN):
                    r, j = divmod(s, CH)
                    load(12 + 3 * a + r, j, [in_cols(j, (COL_Q, COL_K, COL_V)[r] + UNIT * a)])
                    if m is not None:
                        decay_loads(s, None, m)
                    if g is not None:
                        load_bias(s, g)

            sp.dma_start(x_in[:, 0, :].rearrange("p (n c) -> p n c", c=UNIT), x_v[:, 0]).then_inc(x_in_s[0], 16)
            sp.dma_start(rowsA[:, :], conv_w[0, 0:4, :].rearrange("k (t p) -> (k t) p", p=P)).then_inc(rows_in, 16)
            sp.dma_start(rowsB[0:32, :], conv_w[0, 4, :].rearrange("(t p) -> t p", p=P)).then_inc(rows_in, 16)
            sp.dma_start(rowsB[32:64, :], conv_b[0].rearrange("(t p) -> t p", p=P)).then_inc(rows_in, 16)
            sp.dma_start(rowsB[64:80, :], norm_mix_g[0].rearrange("(t p) -> t p", p=P)).then_inc(rows_in, 16)
            sp.dma_start(rowsB[80:96, :], norm_mlp_g[0].rearrange("(t p) -> t p", p=P)).then_inc(rows_in, 16)
            sp.dma_start(rowsB[96:112, :], ssd_norm_g[0].rearrange("(t p) -> t p", p=P)).then_inc(rows_in, 16)
            sp.dma_start(rowsB[112:113, :], q_norm_g[0:1, :]).then_inc(rows_in, 16)
            sp.dma_start(rowsB[113:114, :], k_norm_g[0:1, :]).then_inc(rows_in, 16)
            ssd_window(0, None)
            with sp.Fori(1, 4) as w:
                ssd_window(w, w - 1)
            sp.wait_ge(rel_stored, 32)
            att_window(0, 3, None)
            with sp.Fori(1, 4) as a:
                att_window(a, None, a - 1)
            for n in range(8):
                slab = 1 - n // 4
                for j in range(CH):
                    s = CH * n + j
                    load(OUT_U + n, j, [w_out_v[:, KT * slab + KC * j:KT * slab + KC * (j + 1),
                                                UNIT * (n % 4):UNIT * (n % 4 + 1)]])
                    load_bias(s, 3)
                    if s == 12:
                        sp.wait_ge(chunk_used, CH * MIX_UNITS)
                        for t in range(TT):
                            sp.dma_start(xres[:, :, t, :], x_v[:, t]).then_inc(xres_in, 16)

            def mlp_quarter(q):
                for n in range(4):
                    for j in range(CH):
                        load(MLP_U + 8 * q + n, j, [w_up_v[:, KC * j:KC * (j + 1), ds(2048 * q + UNIT * n, UNIT)]])
                for n in range(4):
                    for j in range(CH):
                        load(MLP_U + 8 * q + 4 + n, j, [w_down_v[:, ds(KT * q + KC * j, KC), UNIT * n:UNIT * (n + 1)]])

            mlp_quarter(0)
            with sp.Fori(1, 4) as q:
                mlp_quarter(q)
            for n in range(4):
                for t in range(TT):
                    sp.wait_ge(down_added, TT * (4 * 3 + n) + t + 1)
                    sp.dma_start(out_v[:, t, n, :], acc[:, n, t, :]).then_inc(out_stored, 16)
            sp.wait_ge(out_stored, 16 * 4 * TT)

        @block.gpsimd
        def _(pool):
            pool.memset(ident[:, :], 1.0).then_inc(consts, 1)
            pool.memset(ones[:, :], 1.0).then_inc(consts, 1)
            pool.memset(halfneg[:, :], -0.5).then_inc(consts, 1)
            pool.memset(relw[:, :], 1.0).then_inc(consts, 1)
            pool.memset(one_row[:, :], 1.0).then_inc(consts, 1)
            pool.memset(prefix[:, :, 0:1], 0.0).then_inc(consts, 1)
            pool.memset(conv_in[:, :, :, 0:2], 0.0).then_inc(consts, 1)
            pool.memset(conv_in[:, :, :, SEQ + 2:SEQ + 4], 0.0).then_inc(consts, 1)
            pool.memset(dtcol[:, 3:4], 1.0).then_inc(consts, 1)
            pool.memset(mask[:, :, :], 1.0).then_inc(consts, 1)
            pool.wait_ge(consts, 10)
            pool.memset(dtcol[0:32, 3:4], -1.0).then_inc(consts, 1)
            pool.wait_ge(consts, 11)
            pool.affine_select(out=ident[:, :], in_=ident[:, :], compare_op=ALU.is_equal, fill=0.0, base=0,
                               pattern=[[-1, P]], channel_multiplier=1).then_inc(pool_masks, 1)
            for i in (0, 2):
                pool.affine_select(out=mask[:, i, :], in_=mask[:, i, :], compare_op=ALU.is_ge, fill=0.0, base=0,
                                   pattern=[[1, P]], channel_multiplier=-1).then_inc(pool_masks, 1)
            for i in (3, 5):
                pool.affine_select(out=mask[:, i, :], in_=mask[:, i, :], compare_op=ALU.is_ge, fill=0.0, base=0,
                                   pattern=[[-1, P]], channel_multiplier=1).then_inc(pool_masks, 1)
            pool.wait_ge(x_ms, 1)
            pool.tensor_tensor(small[:, 4:6], small[:, 2:4], halfneg[:, 0:2], ALU.pow).then_inc(x_rs, 1)

            def low(U, j):
                i = j % RING
                pool.wait_ge(hi_ready, CH * U + j + 1)
                pool.tensor_tensor(w_lo[i][:, :, :], raw[j][:, :, :], w_hi[i][:, :, :].bitcast(f32),
                                   ALU.subtract).then_inc(lo_pool, 1)

            def unit(U):
                for j in POOL_CHUNKS:
                    low(U, j)

            def qk_root(n):
                pool.wait_ge(qk_ms, n + 1)
                pool.tensor_tensor(qk_s[:, 2, :], qk_s[:, 1, :], halfneg[:, :], ALU.pow).then_inc(qk_rs, 1)

            def att_window(a):
                for s in range(WIN):
                    r, j = divmod(s, CH)
                    if j in POOL_CHUNKS:
                        low(12 + 3 * a + r, j)
                    if s == 11 + LEAD:
                        qk_root(2 * a)
                    if s == 19 + LEAD:
                        qk_root(2 * a + 1)

            for U in range(3):
                unit(U)
            with pool.Fori(3, 12) as U:
                unit(U)
            att_window(0)
            with pool.Fori(1, 4) as a:
                att_window(a)
            with pool.Fori(OUT_U, MLP_U + 32) as U:
                unit(U)

        @block.scalar
        def _(act):
            act.dma_start(x_in[:, 1, :].rearrange("p (n c) -> p n c", c=UNIT), x_v[:, 1]).then_inc(x_in_s[1], 16)
            act.wait_ge(consts, 2)
            act.activation(squares_act[:, 0:1], ones[:, 0:1], ACT.Square).then_inc(table_in, 1)
            act.activation(ones_r[:, :], ones[:, :], ACT.Copy).then_inc(ones_rounded, 1)
            act.dma_start(reltab[:, :], bias_table).then_inc(relw_in, 16)
            act.wait_ge(consts, 4)
            act.dma_start(relw[0:BUCKETS, :], rel_bias).then_inc(relw_in, 16)

            act.wait_ge(table_in, 1)
            act.wait_ge(x_in_s[0], 16)
            act.activation(squares_act[:, :], x_in[:, 0, :], ACT.Square, accum_out=small[:, 0:1]).then_inc(x_sq, 1)
            act.wait_ge(x_in_s[1], 16)
            act.wait_ge(x_sq, 1)
            act.activation(squares_act[:, X_SPLIT:], x_in[:, 1, X_SPLIT:], ACT.Square, accum_out=small[:, 44:45]).then_inc(x_sq, 1)

            def x_high(R):
                r = R % 8
                act.wait_ge(xg_ready, R + 1)
                act.activation(actT_hi[:, KC * r:KC * r + KC, :], xg[R % 2][:, :, :], ACT.Copy).then_inc(xh_ready, 1)

            def high(U, j):
                act.wait_ge(raw_in[j], 48 * (U + 1))
                if positive(CH * U + j - RING + 1):
                    act.wait_ge(chunk_used, CH * U + j - RING + 1)
                act.activation(w_hi[j % RING][:, :, :], raw[j][:, :, :], ACT.Copy).then_inc(hi_ready, 1)

            def high_ahead(U0, s):
                n, j = divmod(s + LEAD, CH)
                high(U0 + n, j)

            def xbc_copy(G, i, w):
                act.wait_ge(chunk_used, WIN * w + CH * (i + 1))
                if not isinstance(G, int) or G > 1:
                    act.wait_ge(conv_step, 20 * (G - 1))
                act.wait_ge(consts, 8)
                act.activation(conv_in[:, i, :, 2:2 + SEQ], tiles(i), ACT.Copy).then_inc(xbc_in, 1)

            def z_tanh_of(m):
                act.wait_ge(chunk_used, WIN * (m + 1))
                act.wait_ge(gated, 2 * m + 1)
                act.activation(zs[:, :, :], tiles(2), ACT.Tanh, scale=0.5).then_inc(z_tanh, 1)

            def head_exp(H, h):
                act.wait_ge(args_ready, H + 1)
                act.activation(mix[h][:, :, :], mix[h][:, :, :], ACT.Exp).then_inc(decays_ready, 1)

            def conv_tanh_of(G):
                act.wait_ge(conv_step, 20 * (G + 1))
                act.activation(conv_t[:, :, :], conv[:, :, :], ACT.Tanh).then_inc(conv_tanh, 1)

            def ssd_slot(s, m, more=True):
                for i, o in enumerate(GROUP_SLOT):
                    G, k = 2 * m + i, s - o
                    if k in (0, 1):
                        for h in (2 * k, 2 * k + 1):
                            head_exp(4 * G + h, h)
                    if k == 2:
                        act.wait_ge(x_transposed, G + 1)
                        act.activation(xtok[:, :, :], M0.rearrange("p (t s) -> p t s", t=2), ACT.Copy)\
                            .then_inc(xtok_ready, 1)
                    if k == 8:
                        act.wait_ge(gated, G + 2)
                        act.activation(gate_sq[:, :, :], gate[:, :, :], ACT.Square).then_inc(gate_squared, 1)
                        act.wait_ge(gate_squared, G + 1)
                        act.activation(sq_hi[:, :, :], gate_sq[:, :, :], ACT.Copy).then_inc(sq_high, 1)
                    if k == 8 and (i == 0 or more):
                        conv_tanh_of(G + 1)
                    if k == 10:
                        act.wait_ge(m1_free, G + 2)
                        act.activation(log_ms[:, :], mean_sq[:, :], ACT.Ln).then_inc(ln_ready, 1)
                        act.wait_ge(ln_ready, G + 1)
                        act.activation(rnorm[:, :], log_ms[:, :], ACT.Exp, scale=-0.5).then_inc(rn_ready, 1)
                    if k == 11:
                        act.wait_ge(normed, G + 1)
                        for c in range(2):
                            ins = act.activation(cat_hi[:, ds(KT + 2 * G + c, 1), :], gate_n[:, c:c + 1, :], ACT.Copy,
                                                 scale=parB[:, ds(96 + 2 * G + c, 1)])
                        ins.then_inc(ssd_hi, 1)

            def qk_square(n, i, a):
                act.wait_ge(chunk_used, WIN * (4 + a) + CH * (i + 1))
                if positive(n):
                    act.wait_ge(qk_ss, n)
                act.activation(sq_tmp[:, :, :], bank_pair(i), ACT.Square).then_inc(qk_sq, 1)

            def v_copy(a):
                act.wait_ge(chunk_used, WIN * (5 + a))
                act.wait_ge(att_lo, 4 * a + 1)
                act.activation(v_hi[:, :, :], bank_pair(2), ACT.Copy).then_inc(v_high, 1)

            def att_slot(s, g):
                for h in range(4):
                    H = 4 * g + h
                    if s == h + 1:
                        act.wait_ge(qk_transposed, H + 1)
                        act.activation(qkT_hi[:, h, 0, :], (M0, M1)[h % 2][:, 0:SEQ], ACT.Copy, scale=gqk[:, 0:1])
                        act.activation(qkT_hi[:, h, 1, :], (M0, M1)[h % 2][:, SEQ:2 * SEQ], ACT.Copy)\
                            .then_inc(qkT_high, 1)
                    if s == 6 + 4 * h:
                        act.wait_ge(neg_max, H + 1)
                        for t in range(TT):
                            ins = act.activation(prob[h % 2][:, t, :], prob[h % 2][:, t, :], ACT.Exp,
                                                 bias=soft[:, h % 2, 1, t:t + 1], accum_out=soft[:, h % 2, 2, t:t + 1])
                        ins.then_inc(probs, 1)
                    if s == 8 + 4 * h:
                        act.wait_ge(p_transposed, H + 1)
                        act.activation(pT_hi[:, :, :], M1.rearrange("p (t s) -> p t s", t=2), ACT.Copy)\
                            .then_inc(pT_high, 1)
                    if s == 10 + 4 * h:
                        act.wait_ge(pv_done, H + 1)
                        act.activation(cat_hi[:, ds(H, 1), :], M1[:, 0:SEQ].rearrange("p (o s) -> p o s", o=1),
                                       ACT.Copy).then_inc(att_hi, 1)

            high(0, 0)
            act.wait_ge(rs_spread, 1)
            act.activation(rs_row[:, :], bank_pair(2)[:, 0, 0:SEQ], ACT.Copy).then_inc(rs_row_in, 1)
            high(0, 1)
            for R in range(8):
                x_high(R)
                if R < 2:
                    high(0, R + 2)
                if 2 <= R < CH - 2:
                    high(0, R + 2)
            act.wait_ge(dtw_in, 16)
            act.activation(dt_hi[:, :, :], dt_raw[:, :, :], ACT.Copy).then_inc(dt_hi_ready, 1)
            act.wait_ge(col_in, 32)
            act.activation(dtcol[:, 2:3], dtcol[:, 1:2], ACT.Exp).then_inc(dt_act, 1)
            for s in range(CH - LEAD, WIN):
                high_ahead(0, s)
                if s == 5:
                    act.wait_ge(rel_copied, 1)
                    act.dma_start(rel_rows, relout[:, :]).then_inc(rel_stored, 16)
                if s == 7:
                    act.wait_ge(dt_step, 2)
                    act.activation(dtv["e"][:, :], dtv["e"][:, :], ACT.Exp, scale=-1.0).then_inc(dt_act, 1)
                if s == 8:
                    act.wait_ge(rel_stored, 16)
                    act.dma_start(rel_tiles.rearrange("p h j -> h p j"),
                                  bass.AP(rel_rows.tensor, P - 1, [[512, HEADS], [-1, P], [1, ROW]]))\
                        .then_inc(rel_stored, 16)
                if s == 11:
                    act.wait_ge(dt_step, 20)
                    act.dma_start(decay_rows[0:32, :].rearrange("h (c s) -> h c s", c=TT),
                                  prefix[0:32, :, 1:P + 1]).then_inc(decay_stored, 16)
                    act.dma_start(decay_rows[32:64, :].rearrange("h (c s) -> h c s", c=TT),
                                  prefix[32:64, :, 0:P]).then_inc(decay_stored, 16)
                if s == 10:
                    xbc_copy(0, 0, 0)
                if s == 18:
                    xbc_copy(1, 1, 0)
                if s == GROUP_SLOT[1] + 8:
                    conv_tanh_of(0)


            def ssd_window(w, m):
                for s in range(WIN):
                    high_ahead(3 * w, s)
                    if s == 2:
                        z_tanh_of(m)
                    ssd_slot(s, m)
                    if s == 10:
                        xbc_copy(2 * w, 0, w)
                    if s == 18:
                        xbc_copy(2 * w + 1, 1, w)

            def att_window(a, m, g):
                for s in range(WIN):
                    high_ahead(12 + 3 * a, s)
                    if m is not None:
                        if s == 2:
                            z_tanh_of(m)
                        ssd_slot(s, m, False)
                    if g is not None:
                        if s == 2:
                            v_copy(g)
                        att_slot(s, g)
                    if s == 10:
                        qk_square(2 * a, 0, a)
                    if s == 18:
                        qk_square(2 * a + 1, 1, a)

            with act.Fori(1, 4) as w:
                ssd_window(w, w - 1)
            att_window(0, 3, None)
            with act.Fori(1, 4) as a:
                att_window(a, None, a - 1)
            for n in range(8):
                for j in range(CH):
                    s = CH * n + j
                    high_ahead(OUT_U, s)
                    if s == 2:
                        v_copy(3)
                    att_slot(s, 3)
                    if n > 4 and j == 4:
                        b = n - 5
                        for t in range(TT):
                            act.wait_ge(added, 4 + b + 1)
                            if positive(TT * b + t):
                                act.wait_ge(squared_mid, TT * b + t)
                            act.activation(sq_junk[:, :], acc[:, b, t, :], ACT.Square,
                                           accum_out=ssum[:, t, b:b + 1]).then_inc(squared_mid, 1)
                        x_high(8 + 2 * b)
                        x_high(9 + 2 * b)
            x_high(14)
            x_high(15)
            high(MLP_U, LEAD)
            for t in range(TT):
                act.wait_ge(added, 8)
                act.wait_ge(squared_mid, TT * 3 + t)
                act.activation(sq_junk[:, :], acc[:, 3, t, :], ACT.Square,
                               accum_out=ssum[:, t, 3:4]).then_inc(squared_mid, 1)

            def relu(U, n, q):
                act.wait_ge(chunk_used, CH * (U + 1))
                if positive(4 * q + n):
                    act.wait_ge(relu_squared, 4 * q + n)
                act.activation(relu_t[:, :, :], tiles(n), ACT.Relu).then_inc(relu_done, 1)

            def hid_high(n, q):
                act.wait_ge(relu_squared, 4 * q + n + 1)
                act.activation(hid_hi[:, 4 * n:4 * n + 4, :], relu_sq[:, :, :], ACT.Copy).then_inc(hid_hi_s, 1)

            def mlp_quarter(q, start):
                for s in range(start, 8 * CH):
                    n, j = divmod(s, CH)
                    high(MLP_U + 8 * q + n, j)
                    if 1 <= n <= 4 and j == 2:
                        relu(MLP_U + 8 * q + n - 1, n - 1, q)
                    if 1 <= n <= 4 and j == 3:
                        hid_high(n - 1, q)

            mlp_quarter(0, LEAD + 1)
            with act.Fori(1, 4) as q:
                mlp_quarter(q, 0)

        @block.vector
        def _(dve):
            tt_, ts_, stt_ = dve.tensor_tensor, dve.tensor_scalar, dve.scalar_tensor_tensor
            dve.sem_inc(gated, 1)
            dve.sem_inc(att_lo, 1)
            dve.sem_inc(logits, 2)

            dve.wait_ge(x_in_s[1], 16)
            dve.tensor_tensor_reduce(out=squares_dve[:, 0:X_SPLIT], in0=x_in[:, 1, 0:X_SPLIT], in1=x_in[:, 1, 0:X_SPLIT],
                                     scale=1.0, scalar=0.0, op0=ALU.mult, op1=ALU.add,
                                     accum_out=small[:, 1:2]).then_inc(x_sq_dve, 1)
            dve.wait_ge(x_sq_dve, 1)
            dve.wait_ge(x_sq, 2)
            tt_(small[:, 1:2], small[:, 1:2], small[:, 44:45], ALU.add).then_inc(x_sq_dve, 1)
            dve.wait_ge(x_sq_dve, 2)
            ts_(small[:, 2:4], small[:, 0:2], 1.0 / D_MODEL, EPS, ALU.mult, ALU.add).then_inc(x_ms, 1)
            dve.wait_ge(params_t, 1)
            dve.tensor_copy(parA[:, :], M0[:, 0:P]).then_inc(params_ready, 1)
            dve.tensor_copy(parB[:, :], M0[:, P:P + 114]).then_inc(params_ready, 1)
            dve.wait_ge(x_rs, 1)
            dve.wait_ge(pool_masks, 1)
            for t in range(TT):
                ts_(rs_diag[:, t, :], ident[:, :], small[:, 4 + t:5 + t], None, ALU.mult).then_inc(rs_diagonal, 1)

            def x_gain_root(R):
                dve.wait_ge(xt_done, R + 1)
                if positive(R - 1):
                    dve.wait_ge(xh_ready, R - 1)
                if positive(R - 1):
                    dve.wait_ge(xl_ready, R - 1)
                for k in range(KC):
                    ins = stt_(xg[R % 2][:, k, :], (M0, M1)[R % 2][:, SEQ * k:SEQ * (k + 1)],
                               parB[:, 64 + KC * R + k:65 + KC * R + k], rs_row[:, :], ALU.mult, ALU.mult)
                ins.then_inc(xg_ready, 1)

            def x_gain(R, g0):
                r = R % 8
                dve.wait_ge(xt_done, R + 1)
                if positive(R - 1):
                    dve.wait_ge(xh_ready, R - 1)
                if positive(R - 1):
                    dve.wait_ge(xl_ready, R - 1)
                gain = parB[:, g0 + KC * r:g0 + KC * r + KC].rearrange("p (t o) -> p t o", o=1)\
                    .broadcast_to([P, KC, SEQ])
                tt_(xg[R % 2][:, :, :], (M0, M1)[R % 2].rearrange("p (t s) -> p t s", t=KC), gain, ALU.mult)\
                    .then_inc(xg_ready, 1)

            def x_low(R):
                r = R % 8
                dve.wait_ge(xh_ready, R + 1)
                tt_(actT_lo[:, KC * r:KC * r + KC, :], xg[R % 2][:, :, :],
                    actT_hi[:, KC * r:KC * r + KC, :].bitcast(f32), ALU.subtract).then_inc(xl_ready, 1)

            def low(U, j):
                i = j % RING
                dve.wait_ge(hi_ready, CH * U + j + 1)
                tt_(w_lo[i][:, :, :], raw[j][:, :, :], w_hi[i][:, :, :].bitcast(f32), ALU.subtract).then_inc(lo_dve, 1)

            def low_ahead(U0, s):
                n, j = divmod(s + LEAD, CH)
                if j in DVE_CHUNKS:
                    low(U0 + n, j)

            def decay_args(G, h):
                H, w, rows = 4 * G + h, mix[h], decay
                dve.wait_ge(decay_in, 32 * (G + 1))
                dve.wait_ge(y_done, H + 1)
                f, b = ds(H, 1), ds(32 + H, 1)
                for k, (d, l, src, col) in enumerate((
                        (0, 0, 0, f), (0, 1, 2, f), (0, 1, 1, f), (1, 0, 0, b), (1, 0, 2, b), (1, 1, 1, b))):
                    ins = ts_(w[:, k, :], rows[:, d, h, P * l:P * l + P], tokp[:, src, col], 0.0, ALU.add, ALU.min)
                ins.then_inc(args_ready, 1)

            def mix_head(G, h):
                H, w = 4 * G + h, mix[h]
                dve.wait_ge(decays_ready, H + 1)
                dve.wait_ge(cb_masked, G + 1)
                for k0, k1, src, col in ((0, 2, 3, H), (2, 3, 4, H), (3, 4, 3, 32 + H), (4, 6, 4, 32 + H)):
                    ins = stt_(w[:, k0:k1, :], w[:, k0:k1, :], tokp[:, src, ds(col, 1)], cbm[:, k0:k1, :],
                               ALU.mult, ALU.mult)
                ins.then_inc(scaled, 1)
                dve.wait_ge(scaled, H + 1)
                tt_(w[:, 0:6:5, :], w[:, 0:3:2, :], w[:, 3:6:2, :], ALU.add).then_inc(mix_ready, 1)

            def convolve(G, i, taps):
                dve.wait_ge(xbc_in, G + 1)
                if 0 in taps and positive(G):
                    dve.wait_ge(xbc_ready, G)
                for k in taps:
                    for c in range(4):
                        tile = 2 * G + c if c < 2 else (16 + G if c == 2 else 24 + G)
                        wt = parA[:, ds(32 * k + tile, 1)] if k < 4 else parB[:, ds(tile, 1)]
                        src = conv_in[:, i, c, k:k + SEQ]
                        if k == 0:
                            ts_(conv[:, c, :], src, wt, parB[:, ds(32 + tile, 1)], ALU.mult, ALU.add)\
                                .then_inc(conv_step, 1)
                        else:
                            dve.wait_ge(conv_step, 20 * G + 4 * (k - 1) + c + 1)
                            stt_(conv[:, c, :], src, wt, conv[:, c, :], ALU.mult, ALU.add).then_inc(conv_step, 1)

            def silu(G):
                dve.wait_ge(conv_tanh, G + 1)
                stt_(xbc[:, :, :], conv_t[:, :, :], 1.0, conv[:, :, :], ALU.add, ALU.mult).then_inc(xbc_ready, 1)

            def mask_cb(G):
                dve.wait_ge(cb_done, G + 1)
                cb = M1.rearrange("p (t l) -> p t l", l=P)
                for k0, k1, b in ((0, 2, 0), (2, 3, 3), (3, 4, 0), (4, 6, 2)):
                    ins = tt_(cbm[:, k0:k1, :], cb[:, b:b + k1 - k0, :], mask[:, k0:k1, :], ALU.mult)
                ins.then_inc(cb_masked, 1)

            def gate_group(G, i, m):
                dve.wait_ge(y_done, 4 * G + 8)
                for c in range(2):
                    ins = stt_(gate_t[:, c, :], xbc[:, c, :], dskip[:, ds(2 * G + c, 1)],
                               M0[:, SEQ * c:SEQ * (c + 1)], ALU.mult, ALU.add)
                ins.then_inc(m0_free, 1)
                dve.wait_ge(m0_free, G + 2)
                dve.wait_ge(z_ready, m + 1)
                tt_(gate[:, :, :], gate_t[:, :, :], zs[:, 2 * i:2 * i + 2, :], ALU.mult).then_inc(gated, 1)

            def group_mean(G):
                dve.wait_ge(norm_summed, G + 1)
                ts_(mean_sq[:, :], M1[:, 0:SEQ], 1.0 / (4 * 256), EPS, ALU.mult, ALU.add).then_inc(m1_free, 1)

            def group_norm(G):
                dve.wait_ge(rn_ready, G + 1)
                stt_(newton[:, :], rnorm[:, :], -0.5, rnorm[:, :], ALU.mult, ALU.mult).then_inc(newton_step, 1)
                dve.wait_ge(newton_step, 3 * G + 1)
                dve.wait_ge(m1_free, G + 2)
                tt_(newton[:, :], newton[:, :], mean_sq[:, :], ALU.mult).then_inc(newton_step, 1)
                dve.wait_ge(newton_step, 3 * G + 2)
                stt_(rnorm[:, :], newton[:, :], 1.5, rnorm[:, :], ALU.add, ALU.mult).then_inc(newton_step, 1)
                dve.wait_ge(newton_step, 3 * G + 3)
                rb = rnorm[:, :].rearrange("p (o s) -> p o s", o=1).broadcast_to([P, 2, SEQ])
                tt_(gate_n[:, :, :], gate[:, :, :], rb, ALU.mult).then_inc(normed, 1)

            def group_low(G):
                dve.wait_ge(normed, G + 1)
                dve.wait_ge(ssd_hi, G + 1)
                for c in range(2):
                    k = ds(KT + 2 * G + c, 1)
                    ins = stt_(cat_lo[:, k, :], gate_n[:, c:c + 1, :], parB[:, ds(96 + 2 * G + c, 1)],
                               cat_hi[:, k, :].bitcast(f32), ALU.mult, ALU.subtract)
                ins.then_inc(ssd_lo, 1)

            def z_silu(m):
                dve.wait_ge(z_tanh, m + 1)
                stt_(zs[:, :, :], zs[:, :, :], 1.0, tiles(2), ALU.add, ALU.mult).then_inc(z_ready, 1)

            def next_group(G, k):
                if k == 9:
                    silu(G)
                if 8 <= k < 12:
                    decay_args(G, k - 8)

            def ssd_slot(s, m, more=True):
                for i, o in enumerate(GROUP_SLOT):
                    G, k = 2 * m + i, s - o
                    if k == 2:
                        mask_cb(G)
                    if 2 <= k < 6:
                        mix_head(G, k - 2)
                    if k == 8:
                        gate_group(G, i, m)
                    if k == 8:
                        dve.wait_ge(sq_high, G + 1)
                        tt_(sq_lo[:, :, :], gate_sq[:, :, :], sq_hi[:, :, :].bitcast(f32), ALU.subtract)\
                            .then_inc(sq_low, 1)
                    if k == 9:
                        group_mean(G)
                    if k == 10:
                        group_norm(G)
                    if k == 11:
                        group_low(G)
                    if k in CONV_SLOTS and (i == 0 or more):
                        convolve(G + 1, 1 - i, CONV_SLOTS[k])
                    if i == 0 or more:
                        next_group(G + 1, k)
                if s == 2:
                    z_silu(m)

            def qk_sum(n):
                dve.wait_ge(qk_sq, n + 1)
                sq = sq_tmp[:, :, :].rearrange("p t (h e) -> p (t h) e", e=HEAD_DIM)
                dve.tensor_reduce(qk_s[:, 0, :], sq, axis=AX.X, op=ALU.add).then_inc(qk_ss, 1)
                dve.wait_ge(qk_ss, n + 1)
                ts_(qk_s[:, 1, :], qk_s[:, 0, :], 1.0 / HEAD_DIM, EPS, ALU.mult, ALU.add).then_inc(qk_ms, 1)

            def qk_norm(n, i, a):
                dve.wait_ge(qk_rs, n + 1)
                if positive(4 * a):
                    dve.wait_ge(qk_transposed, 4 * a)
                rs = qk_s[:, 2, :].rearrange("p (h o) -> p h o", o=1).broadcast_to([P, 8, HEAD_DIM])
                tt_(qk_n[i][:, :, :].rearrange("p t (h e) -> p (t h) e", e=HEAD_DIM),
                    bank_pair(i).rearrange("p t (h e) -> p (t h) e", e=HEAD_DIM), rs, ALU.mult).then_inc(qk_normed, 1)

            def att_slot(s, g):
                if s == 2:
                    dve.wait_ge(v_high, g + 1)
                    tt_(v_lo[:, :, :], bank_pair(2), v_hi[:, :, :].bitcast(f32), ALU.subtract).then_inc(v_low, 1)
                for h in range(4):
                    H = 4 * g + h
                    i = h % 2
                    if s == h + 1:
                        dve.wait_ge(qkT_high, H + 1)
                        stt_(qkT_lo[:, h, 0, :], (M0, M1)[i][:, 0:SEQ], gqk[:, 0:1],
                             qkT_hi[:, h, 0, :].bitcast(f32), ALU.mult, ALU.subtract)
                        tt_(qkT_lo[:, h, 1, :], (M0, M1)[i][:, SEQ:2 * SEQ], qkT_hi[:, h, 1, :].bitcast(f32),
                            ALU.subtract).then_inc(qkT_ready, 1)
                    if s == 5 + 4 * h:
                        dve.wait_ge(scores, H + 1)
                        dve.wait_ge(bias_in[i], 16 * (2 * g + h // 2 + 1))
                        dve.memset(small[:, 40:41], 0.0)
                        for t in range(TT):
                            ins = dve.tensor_tensor_reduce(
                                out=prob[i][:, t, :], in0=M0[:, SEQ * t:SEQ * (t + 1)],
                                in1=bias_t[i][:, P * (1 - t):P * (1 - t) + SEQ], scale=1.0, scalar=-3e38,
                                op0=ALU.add, op1=ALU.max, accum_out=soft[:, i, 0, t:t + 1])
                        ins.then_inc(logits, 1)
                        dve.wait_ge(logits, H + 3)
                        ts_(soft[:, i, 1, :], soft[:, i, 0, :], -1.0, None, ALU.mult).then_inc(neg_max, 1)
                    if s == 6 + 4 * h:
                        dve.wait_ge(probs, H + 1)
                        dve.reciprocal(soft[:, i, 3, :], soft[:, i, 2, :]).then_inc(recip, 1)
                        dve.wait_ge(recip, H + 1)
                        for t in range(TT):
                            ins = ts_(prob[i][:, t, :], prob[i][:, t, :], soft[:, i, 3, t:t + 1], None, ALU.mult)
                        ins.then_inc(p_normed, 1)
                    if s == 8 + 4 * h:
                        dve.wait_ge(pT_high, H + 1)
                        tt_(pT_lo[:, :, :], M1.rearrange("p (t s) -> p t s", t=2), pT_hi[:, :, :].bitcast(f32),
                            ALU.subtract).then_inc(pT_ready, 1)
                    if s == 10 + 4 * h:
                        dve.wait_ge(att_hi, H + 1)
                        tt_(cat_lo[:, ds(H, 1), :], M1[:, 0:SEQ].rearrange("p (o s) -> p o s", o=1),
                            cat_hi[:, ds(H, 1), :].bitcast(f32), ALU.subtract).then_inc(att_lo, 1)

            dve.wait_ge(rs_row_in, 1)
            dve.wait_ge(params_ready, 2)
            for R in range(8):
                x_gain_root(R)
                if R > 0:
                    x_low(R - 1)
                if R == 3:
                    low(0, 3)
            low(0, 7)
            x_low(7)
            dve.wait_ge(params_ready, 2)
            ts_(parA[:, :], parA[:, :], 0.5, None, ALU.mult).then_inc(params_ready, 1)
            ts_(parB[:, 0:64], parB[:, 0:64], 0.5, None, ALU.mult).then_inc(params_ready, 1)
            ts_(parB[:, 96:112], parB[:, 96:112], 0.5, None, ALU.mult).then_inc(params_ready, 1)
            ts_(gqk[:, :], parB[:, 112:113], parB[:, 113:114], 1.0 / math.sqrt(HEAD_DIM), ALU.mult, ALU.mult)\
                .then_inc(params_ready, 1)
            dve.wait_ge(dskip_in, 16)
            for i in range(2):
                dve.tensor_copy(dskip[64 * i:64 * i + 64, :], dskip_all[64 * i:64 * i + 64, i:SSM_HEADS:2])\
                    .then_inc(params_ready, 1)
            dve.wait_ge(rel_done, 1)
            dve.tensor_copy(relout[:, :], M1[0:HEADS, :]).then_inc(rel_copied, 1)
            dve.wait_ge(dt_hi_ready, 1)
            tt_(dt_lo[:, :, :], dt_raw[:, :, :], dt_hi[:, :, :].bitcast(f32), ALU.subtract).then_inc(dt_lo_ready, 1)
            dve.wait_ge(dt_act, 1)
            ts_(dtcol[:, 4:5], dtcol[:, 2:3], dtcol[:, 3:4], None, ALU.mult).then_inc(dt_step, 1)
            v, e, r, z, z2, p, soft_dt, a_dt = (dtv[n][:, :] for n in ("v", "e", "r", "z", "z2", "p", "soft", "a"))
            step = [1]

            def then_step(ins):
                ins.then_inc(dt_step, 1)
                step[0] += 1
                dve.wait_ge(dt_step, step[0])

            def dt_softplus():
                dve.wait_ge(dt_done, 1)
                ts_(v, M0[0:64, 0:SEQ], dtcol[:, 0:1], None, ALU.add).then_inc(m0_free, 1)
                dve.wait_ge(m0_free, 1)
                then_step(stt_(e, v, -1.0, v, ALU.mult, ALU.max))
                dve.wait_ge(dt_act, 2)
                then_step(ts_(r, e, 2.0, None, ALU.add))
                then_step(dve.reciprocal(r, r))
                then_step(tt_(z, e, r, ALU.mult))
                then_step(tt_(z2, z, z, ALU.mult))
                then_step(ts_(p, z2, 1.0 / 17, None, ALU.mult))
                for k in (15, 13, 11, 9, 7, 5, 3):
                    then_step(stt_(p, p, 1.0 / k, z2, ALU.add, ALU.mult))
                then_step(stt_(p, p, 1.0, z, ALU.add, ALU.mult))
                then_step(ts_(r, v, 0.0, None, ALU.max))
                then_step(stt_(soft_dt, p, 2.0, r, ALU.mult, ALU.add))
                then_step(ts_(a_dt, soft_dt, dtcol[:, 4:5], None, ALU.mult))

            def dt_sums():
                for c in range(TT):
                    then_step(dve.tensor_tensor_scan(prefix[:, c, 1:P + 1], one_row[:, :], a_dt[:, P * c:P * (c + 1)],
                                                     0.0, ALU.mult, ALU.add))
                F, B = slice(0, 32), slice(32, 64)
                for c in range(TT):
                    ts_(dt_rows[F, c, :], prefix[F, c, 1:P + 1], -1.0, None, ALU.mult)
                    ts_(dt_rows[B, c, :], prefix[B, c, 0:P], -1.0, None, ALU.mult)
                    dve.tensor_copy(dt_rows[:, 3 + c, :], soft_dt[:, P * c:P * (c + 1)])
                ts_(dt_rows[F, 2, :], prefix[F, 0, 1:P + 1], -1.0, prefix[F, 0, P:P + 1], ALU.mult, ALU.add)
                then_step(ts_(dt_rows[B, 2, :], prefix[B, 1, 0:P], -1.0, prefix[B, 0, P:P + 1], ALU.mult, ALU.subtract))

            def dt_tokens():
                dve.wait_ge(dt_tok, 1)
                dve.tensor_copy(tokp[:, :, :].rearrange("p a h -> p (a h)"), M1[:, 0:320]).then_inc(m1_free, 1)

            for s in range(CH - LEAD, WIN):
                low_ahead(0, s)
                if s == 6:
                    dt_softplus()
                if s == 8:
                    dt_sums()
                if s == 13:
                    dt_tokens()
                if s - GROUP_SLOT[1] in CONV_SLOTS:
                    if s - GROUP_SLOT[1] == 0:
                        dve.wait_ge(params_ready, 8)
                    convolve(0, 0, CONV_SLOTS[s - GROUP_SLOT[1]])
                next_group(0, s - GROUP_SLOT[1])
            dve.wait_ge(pool_masks, 5)
            dve.wait_ge(m1_free, 1)
            dve.wait_ge(params_ready, 8)

            def ssd_window(w, m):
                for s in range(WIN):
                    low_ahead(3 * w, s)
                    ssd_slot(s, m)

            def att_window(a, m, g):
                for s in range(WIN):
                    low_ahead(12 + 3 * a, s)
                    if m is not None:
                        ssd_slot(s, m, False)
                    if g is not None:
                        att_slot(s, g)
                    for i in range(2):
                        if s == 10 + 8 * i:
                            qk_sum(2 * a + i)
                        if s == 12 + 8 * i:
                            qk_norm(2 * a + i, i, a)

            with dve.Fori(1, 4) as w:
                ssd_window(w, w - 1)
            att_window(0, 3, None)
            with dve.Fori(1, 4) as a:
                att_window(a, None, a - 1)

            def out_add(n):
                dve.wait_ge(chunk_used, CH * (OUT_U + n + 1))
                dve.wait_ge(xres_in, 32)
                if n < 4:
                    tt_(xres[:, n], bank_pair((0, 1, 2, 0)[n]), xres[:, n], ALU.add).then_inc(added, 1)
                else:
                    tt_(acc[:, n - 4], bank_pair((1, 2, 0, 1)[n - 4]), xres[:, n - 4], ALU.add).then_inc(added, 1)

            def mid_block(b):
                for R in (8 + 2 * b, 9 + 2 * b):
                    x_gain(R, 80)
                for R in (8 + 2 * b, 9 + 2 * b):
                    x_low(R)

            for n in range(8):
                for j in range(CH):
                    s = CH * n + j
                    low_ahead(OUT_U, s)
                    att_slot(s, 3)
                    if n > 0 and j == 2:
                        out_add(n - 1)
                    if n > 4 and j == 4:
                        mid_block(n - 5)
            out_add(7)
            mid_block(3)
            low(MLP_U, DVE_CHUNKS[0])
            dve.wait_ge(squared_mid, 8)
            dve.tensor_reduce(inv_ms[:, 0, :], ssum[:, :, :], axis=AX.X, op=ALU.add).then_inc(mid_step, 1)
            dve.wait_ge(mid_step, 1)
            ts_(inv_ms[:, 1, :], inv_ms[:, 0, :], 1.0 / D_MODEL, EPS, ALU.mult, ALU.add).then_inc(mid_step, 1)
            dve.wait_ge(mid_step, 2)
            dve.reciprocal(inv_ms[:, 2, :], inv_ms[:, 1, :]).then_inc(mid_step, 1)
            dve.wait_ge(mid_step, 3)

            def relu_square(n, q):
                dve.wait_ge(relu_done, 4 * q + n + 1)
                if positive(4 * q + n):
                    dve.wait_ge(hid_hi_s, 4 * q + n)
                if positive(4 * q + n):
                    dve.wait_ge(hid_lo_s, 4 * q + n)
                tt_(relu_sq[:, :, :], relu_t[:, :, :], relu_t[:, :, :], ALU.mult).then_inc(relu_squared, 1)

            def hid_low(n, q):
                dve.wait_ge(hid_hi_s, 4 * q + n + 1)
                tt_(hid_lo[:, 4 * n:4 * n + 4, :], relu_sq[:, :, :], hid_hi[:, 4 * n:4 * n + 4, :].bitcast(f32),
                    ALU.subtract).then_inc(hid_lo_s, 1)

            def down_add(U, n, q):
                dve.wait_ge(chunk_used, CH * (U + 1))
                if positive(4 * (q - 1) + n + 1):
                    dve.wait_ge(down_added, TT * (4 * (q - 1) + n + 1))
                for t in range(TT):
                    stt_(acc[:, n, t, :], bank_pair(n)[:, t, :], inv_ms[:, 2, t:t + 1], acc[:, n, t, :],
                         ALU.mult, ALU.add).then_inc(down_added, 1)

            def mlp_quarter(q, start):
                for s in range(start, 8 * CH):
                    n, j = divmod(s, CH)
                    if j in DVE_CHUNKS:
                        low(MLP_U + 8 * q + n, j)
                    if 1 <= n <= 4 and j == 2:
                        relu_square(n - 1, q)
                    if 1 <= n <= 4 and j == 3:
                        hid_low(n - 1, q)
                    if n >= 5 and j == 2:
                        down_add(MLP_U + 8 * q + n - 1, n - 5, q)
                down_add(MLP_U + 8 * q + 7, 3, q)

            mlp_quarter(0, DVE_CHUNKS[0] + 1)
            with dve.Fori(1, 4) as q:
                mlp_quarter(q, 0)

        @block.tensor
        def _(pe):
            def mm(o, lhsT, rhs, first, last, **kw):
                return pe.matmul(o, lhsT, rhs, start=first, stop=last, **kw)

            pe.sem_inc(y_done, PER_GROUP)

            def chunk_by_weights(U, j, pair, skip=False):
                wait_low(pe, U, j)
                i = j % RING
                res = tiles(pair)
                for kk in range(KC):
                    k = KC * j + kk
                    for c in range(4):
                        cols = slice(P * c, P * c + P)
                        for n, (w, a) in enumerate(((w_hi, actT_lo), (w_lo, actT_hi), (w_hi, actT_hi))):
                            ins = mm(res[:, c, :], w[i][:, kk, cols], a[:, k, :],
                                     k == 0 and n == 0 and c % 2 == 0,
                                     k == KT - 1 and n == 2, skip_group_check=True)
                ins.then_inc(chunk_used, 1)

            def chunk_by_tokens(U, j, pair, hi, lo, k0):
                wait_low(pe, U, j)
                i = j % RING
                for kk in range(KC):
                    k = KC * j + kk
                    for t in range(TT):
                        toks = slice(P * t, P * t + P)
                        for n, (a, w) in enumerate(((lo, w_hi), (hi, w_lo), (hi, w_hi))):
                            ins = mm(bank_pair(pair)[:, t, :], a[:, k0 + k, toks], w[i][:, kk, :],
                                     k == 0 and n == 0, k == KT - 1 and n == 2)
                ins.then_inc(chunk_used, 1)

            def rows_round(R):
                r = R % 8
                bank = (M0, M1)[R % 2]
                if positive(R - 1):
                    pe.wait_ge(xg_ready, R - 1)
                for kk in range(KC):
                    for t in range(TT):
                        k = KC * r + kk
                        src = (x_in[:, t, P * k:P * k + P] if R < 8 else
                               acc[:, k // 4, t, P * (k % 4):P * (k % 4) + P])
                        ins = pe.transpose(bank[:, SEQ * kk + P * t:SEQ * kk + P * t + P], src, ident[:, :])
                ins.then_inc(xt_done, 1)

            def ssd_slot(s, m):
                for i, o in enumerate(GROUP_SLOT):
                    G, k = 2 * m + i, s - o
                    if k == 1:
                        pe.wait_ge(xbc_ready, G + 1)
                        pe.wait_ge(m0_free, G + 1)
                        for t in range(TT):
                            for c in range(2):
                                ins = pe.transpose(M0[:, SEQ * t + P * c:SEQ * t + P * c + P],
                                                   xbc[:, c, P * t:P * t + P], ident[:, :])
                        ins.then_inc(x_transposed, 1)
                        pe.wait_ge(m1_free, G + 1)
                        for t in range(TT):
                            ins = mm(M1[:, SEQ * t:SEQ * (t + 1)], xbc[:, 2, P * t:P * t + P], xbc[:, 3, :], True, True)
                        ins.then_inc(cb_done, 1)
                    if k in (5, 7):
                        pe.wait_ge(xtok_ready, G + 1)
                        pe.wait_ge(mix_ready, 4 * G + k - 3)
                        for t in range(TT):
                            for h in (k - 5, k - 4):
                                ins = mm(M0[64 * (h % 2):64 * (h % 2) + 64, SEQ * (h // 2):SEQ * (h // 2 + 1)],
                                         xtok[:, t, 64 * h:64 * h + 64], mix[h][:, 4 * t:4 * t + 2, :],
                                         t == 0, t == TT - 1)
                                if t == TT - 1:
                                    ins.then_inc(y_done, 1)
                    if k == 9:
                        pe.wait_ge(sq_low, G + 1)
                        pe.wait_ge(ones_rounded, 1)
                        pe.wait_ge(cb_masked, G + 1)
                        for c in range(2):
                            mm(M1[:, 0:SEQ], ones_r[:, :], sq_lo[:, c, :], c == 0, False)
                            ins = mm(M1[:, 0:SEQ], ones_r[:, :], sq_hi[:, c, :], False, c == 1)
                        ins.then_inc(norm_summed, 1)

            def att_slot(s, g):
                for h in range(4):
                    H = 4 * g + h
                    if s == h:
                        pe.wait_ge(qk_normed, 2 * g + 2)
                        if h == 0:
                            pe.wait_ge(m0_free, 9)
                            pe.wait_ge(logits, 4 * g + 2)
                        if h == 1:
                            pe.wait_ge(m1_free, 9)
                            pe.wait_ge(att_lo, 4 * g + 1)
                        if h > 1:
                            pe.wait_ge(qkT_ready, H - 1)
                        for n in range(2):
                            for t in range(TT):
                                ins = pe.transpose((M0, M1)[h % 2][:, SEQ * n + P * t:SEQ * n + P * t + P],
                                                   qk_n[n][:, t, P * h:P * h + P], ident[:, :])
                        ins.then_inc(qk_transposed, 1)
                    if s == 4 + 4 * h:
                        pe.wait_ge(qkT_ready, 4 * g + max(h + 1, 3))
                        if h > 0:
                            pe.wait_ge(logits, H + 2)
                        for t in range(TT):
                            for n, (q, k) in enumerate(((qkT_lo, qkT_hi), (qkT_hi, qkT_lo), (qkT_hi, qkT_hi))):
                                ins = mm(M0[:, SEQ * t:SEQ * (t + 1)], q[:, h, 0, P * t:P * t + P], k[:, h, 1, :],
                                         n == 0, n == 2)
                        ins.then_inc(scores, 1)
                    if s == 7 + 4 * h:
                        pe.wait_ge(p_normed, H + 1)
                        if h == 0:
                            pe.wait_ge(qkT_ready, 4 * g + 4)
                        else:
                            pe.wait_ge(att_lo, H + 1)
                        for n in range(TT):
                            for t in range(TT):
                                ins = pe.transpose(M1[:, SEQ * n + P * t:SEQ * n + P * t + P],
                                                   prob[h % 2][:, t, P * n:P * n + P], ident[:, :])
                        ins.then_inc(p_transposed, 1)
                    if s == 9 + 4 * h:
                        pe.wait_ge(pT_ready, H + 1)
                        pe.wait_ge(v_low, g + 1)
                        for t in range(TT):
                            for n, (v, p) in enumerate(((v_lo, pT_hi), (v_hi, pT_lo), (v_hi, pT_hi))):
                                ins = mm(M1[:, 0:SEQ], v[:, t, P * h:P * h + P], p[:, t, :],
                                         t == 0 and n == 0, t == TT - 1 and n == 2)
                        ins.then_inc(pv_done, 1)

            pe.wait_ge(pool_masks, 1)
            pe.wait_ge(consts, 11)
            pe.wait_ge(rows_in, 128)
            pe.transpose(M0[:, 0:P], rowsA[:, :], ident[:, :])
            pe.transpose(M0[:, P:P + 114], rowsB[:, :], ident[0:114, 0:114]).then_inc(params_t, 1)
            pe.wait_ge(params_ready, 2)
            for R in range(3):
                if R == 0:
                    pe.wait_ge(x_in_s[0], 16)
                    pe.wait_ge(x_in_s[1], 16)
                rows_round(R)
                if R == 0:
                    pe.wait_ge(consts, 2)
                    pe.wait_ge(rs_diagonal, 2)
                    for t in range(TT):
                        ins = mm(bank_pair(2)[:, 0, P * t:P * (t + 1)], ones[:, :], rs_diag[:, t, :], True, True)
                    ins.then_inc(rs_spread, 1)

            def dt_unit():
                pe.wait_ge(xg_ready, 8)
                pe.wait_ge(dt_lo_ready, 1)
                for k in range(KT):
                    for n, (w, a) in enumerate(((dt_hi, actT_lo), (dt_lo, actT_hi), (dt_hi, actT_hi))):
                        ins = mm(M0[0:64, 0:SEQ], w[:, k, :], a[:, k, :], k == 0 and n == 0, k == KT - 1 and n == 2)
                ins.then_inc(dt_done, 1)

            for s in range(WIN):
                r, j = divmod(s, CH)
                if s < CH:
                    pe.wait_ge(xl_ready, j + 1)
                chunk_by_weights(r, j, r)
                if s + 3 < CH:
                    rows_round(s + 3)
                if s == 5:
                    pe.wait_ge(relw_in, 32)
                    pe.wait_ge(xg_ready, 8)
                    mm(M1[0:HEADS, :], relw[:, :], reltab[:, :], True, True).then_inc(rel_done, 1)
                if s == 6:
                    dt_unit()
                if s == 12:
                    pe.wait_ge(rel_copied, 1)
                    pe.wait_ge(dt_step, DT_STEPS)
                    for i in range(5):
                        ins = pe.transpose(M1[:, 64 * i:64 * i + 64], dt_rows[:, i, :], ident[0:64, 0:64])
                    ins.then_inc(dt_tok, 1)

            def ssd_window(w, m):
                for s in range(WIN):
                    r, j = divmod(s, CH)
                    if j == 0:
                        if r < 2:
                            pe.wait_ge(xbc_in, 2 * (w - 1) + r + 1)
                        else:
                            pe.wait_ge(z_ready, w)
                    chunk_by_weights(3 * w + r, j, r)
                    ssd_slot(s, m)

            def att_window(a, m, g):
                for s in range(WIN):
                    r, j = divmod(s, CH)
                    if j == 0:
                        if m is not None:
                            pe.wait_ge((xbc_in, xbc_in, z_ready)[r], (7, 8, 4)[r])
                        elif r < 2:
                            pe.wait_ge(qk_normed, 2 * (a - 1) + r + 1)
                        else:
                            pe.wait_ge(v_low, a)
                    chunk_by_tokens(12 + 3 * a + r, j, r, actT_hi, actT_lo, 0)
                    if m is not None:
                        ssd_slot(s, m)
                    if g is not None:
                        att_slot(s, g)

            with pe.Fori(1, 4) as w:
                ssd_window(w, w - 1)
            att_window(0, 3, None)
            with pe.Fori(1, 4) as a:
                att_window(a, None, a - 1)
            for n in range(8):
                pair = (0, 1, 2, 0, 1, 2, 0, 1)[n]
                for j in range(CH):
                    s = CH * n + j
                    if j == 0:
                        if n < 2:
                            pe.wait_ge(qk_normed, 6 + n + 1)
                        elif n == 2:
                            pe.wait_ge(v_low, 4)
                        else:
                            pe.wait_ge(added, n - 2)
                    if n == 0 and j == 0:
                        pe.wait_ge(ssd_lo, 8)
                    if n == 4:
                        pe.wait_ge(att_lo, 2 * j + 3)
                    chunk_by_tokens(OUT_U + n, j, pair, cat_hi, cat_lo, KT * (1 - n // 4))
                    att_slot(s, 3)
                    if n > 4 and j == 3:
                        pe.wait_ge(added, n)
                        pe.wait_ge(logits, 18)
                        rows_round(8 + 2 * (n - 5))
                        rows_round(9 + 2 * (n - 5))

            def mlp_quarter(q, first):
                for n in range(4):
                    for j in range(CH):
                        if j == 0:
                            if first:
                                if n == 3:
                                    pe.wait_ge(xg_ready, 16)
                                else:
                                    pe.wait_ge(added, 7 + min(n, 1))
                            else:
                                if positive(4 * (q - 1) + n + 1):
                                    pe.wait_ge(down_added, TT * (4 * (q - 1) + n + 1))
                        if first and n == 0 and j == 1:
                            pe.wait_ge(added, 8)
                            rows_round(14)
                            rows_round(15)
                        if first and n == 0:
                            pe.wait_ge(xl_ready, 8 + j + 1)
                        chunk_by_weights(MLP_U + 8 * q + n, j, n)
                for n in range(4):
                    for j in range(CH):
                        if j == 0:
                            pe.wait_ge(relu_done, 4 * q + n + 1)
                        if n == 0 and j % 2 == 0:
                            pe.wait_ge(hid_lo_s, 4 * q + j // 2 + 1)
                        chunk_by_tokens(MLP_U + 8 * q + 4 + n, j, n, hid_hi, hid_lo, 0)

            mlp_quarter(0, True)
            with pe.Fori(1, 4) as q:
                mlp_quarter(q, False)



_INS = ["x", "norm_mix_g", "w_in", "q_norm_g", "k_norm_g", "rel_bias", "conv_w", "conv_b", "dt_bias", "a_log",
        "d_skip", "ssd_norm_g", "w_out", "norm_mlp_g", "w_up", "w_down"]


def kernel(**inputs):
    import concourse.bacc as bacc
    from concourse.bass_utils import run_bass_kernel_spmd

    nc = bacc.Bacc("TRN2", target_bir_lowering=False, num_devices=1)
    arrays, args = {}, []
    for name in _INS:
        a = np.ascontiguousarray(inputs[name])
        arrays[f"in_{name}"] = a
        args.append(nc.dram_tensor(f"in_{name}", a.shape, mybir.dt.from_np(a.dtype), kind="ExternalInput").ap())
    table = bias_constants()
    arrays["bias_table"] = table
    args.append(nc.dram_tensor("bias_table", table.shape, mybir.dt.float32, kind="ExternalInput").ap())
    out = nc.dram_tensor("out", (1, SEQ, D_MODEL), mybir.dt.float32, kind="ExternalOutput").ap()
    build(nc, *args, out)
    r = run_bass_kernel_spmd(nc, [arrays], core_ids=[0])
    return r.results[0]["out"]
```
